# Optimizing a Trainium2 kernel written in Bass

```python
import jax, jax.numpy as jnp
from jax import lax
import numpy as np

D_MODEL = 1024
BATCH = 1
SEQ = 256
DEPTH = 2

N_CONV_LAYERS = DEPTH // 2
N_ATTN_LAYERS = DEPTH - N_CONV_LAYERS
CONV_WIDTH = 3
HEAD_DIM = 64
N_HEADS = D_MODEL // HEAD_DIM
BRANCHES = ((128, 1), (512, 4), (2048, 16))
N_BRANCHES = len(BRANCHES)
Q_WIDTH = N_BRANCHES * N_HEADS * HEAD_DIM
D_FF = -(-8 * D_MODEL // (3 * 256)) * 256
ROPE_THETA = 10000.0
RMS_EPS = 1e-6
NEG_INF = -1e30


def rms_norm(x, g):
    xf = x.astype(jnp.float32)
    y = xf * lax.rsqrt(jnp.mean(xf * xf, axis=-1, keepdims=True) + RMS_EPS)
    return (y * g.astype(jnp.float32)).astype(x.dtype)

def rope(t, positions):
    half = HEAD_DIM // 2
    inv_freq = ROPE_THETA ** (-jnp.arange(half, dtype=jnp.float32) / half)
    ang = positions.astype(jnp.float32)[..., None] * inv_freq
    cos = jnp.cos(ang)[:, :, None, :]
    sin = jnp.sin(ang)[:, :, None, :]
    t1 = t[..., :half].astype(jnp.float32)
    t2 = t[..., half:].astype(jnp.float32)
    out = jnp.concatenate([t1 * cos - t2 * sin, t2 * cos + t1 * sin], axis=-1)
    return out.astype(t.dtype)

def short_conv_mixer(x, w_in, conv_w, w_out):
    b_gate, c_gate, h = jnp.split(x @ w_in, 3, axis=-1)
    u = c_gate * h
    rhs = conv_w[:, None, :].astype(u.dtype)
    conv = lax.conv_general_dilated(
        u, rhs, window_strides=(1,), padding=[(CONV_WIDTH - 1, 0)],
        dimension_numbers=("NWC", "WIO", "NWC"), feature_group_count=u.shape[-1])
    return (b_gate * conv) @ w_out

def swiglu(x, w_gate_up, w_down):
    g, u = jnp.split(x @ w_gate_up, 2, axis=-1)
    return (jax.nn.silu(g) * u) @ w_down

def dilated_branch(q, k, v, window, dilation):
    band = window // dilation
    B, S, H, Dh = q.shape
    chunk = dilation * band
    Sp = -(-S // chunk) * chunk
    nb = Sp // chunk
    pad = ((0, 0), (0, Sp - S), (0, 0), (0, 0))

    def to_blocks(t):
        t = jnp.pad(t, pad).reshape(B, nb, band, dilation, H, Dh)
        return t.transpose(0, 3, 4, 1, 2, 5)

    def with_prev(t):
        prev = jnp.pad(t, ((0, 0), (0, 0), (0, 0), (1, 0), (0, 0), (0, 0)))[:, :, :, :-1]
        return jnp.concatenate([prev, t], axis=4)

    qb = to_blocks(q * (HEAD_DIM ** -0.5))
    kk = with_prev(to_blocks(k))
    vv = with_prev(to_blocks(v))
    s = jnp.einsum("brhnqd,brhnkd->brhnqk", qb, kk).astype(jnp.float32)
    qi = jnp.arange(band)[:, None]
    kj = jnp.arange(2 * band)[None, :]
    dist = qi + band - kj
    in_band = (dist >= 0) & (dist <= band)
    has_prev = (kj >= band)[None] | (jnp.arange(nb)[:, None, None] > 0)
    mask = in_band[None] & has_prev
    s = jnp.where(mask, s, NEG_INF)
    m = jnp.max(s, axis=-1)
    p = jnp.exp(s - m[..., None])
    l = jnp.sum(p, axis=-1)
    o = jnp.einsum("brhnqk,brhnkd->brhnqd", p, vv.astype(jnp.float32)) / l[..., None]
    lse = m + jnp.log(l)
    o = o.transpose(0, 3, 4, 1, 2, 5).reshape(B, Sp, H, Dh)[:, :S]
    lse = lse.transpose(0, 3, 4, 1, 2).reshape(B, Sp, H)[:, :S]
    return o, lse

def dilated_attention_mixer(x, positions, k_sh, v_sh, w_q, w_o):
    B, S, _ = x.shape
    q = (x @ w_q).reshape(B, S, N_BRANCHES * N_HEADS, HEAD_DIM)
    q = rope(q, positions).reshape(B, S, N_BRANCHES, N_HEADS, HEAD_DIM)
    outs, lses = [], []
    for g, (window, dilation) in enumerate(BRANCHES):
        o, lse = dilated_branch(q[:, :, g], k_sh[:, :, g], v_sh[:, :, g], window, dilation)
        outs.append(o)
        lses.append(lse)
    wts = jax.nn.softmax(jnp.stack(lses, axis=0), axis=0)
    o = jnp.einsum("gbsh,gbshd->bshd", wts, jnp.stack(outs, axis=0))
    return o.astype(x.dtype).reshape(B, S, N_HEADS * HEAD_DIM) @ w_o

def shared_kv(h, positions, kv_norm, w_kv):
    B, S, _ = h.shape
    kv = (rms_norm(h, kv_norm) @ w_kv).reshape(B, S, 2, N_BRANCHES * N_HEADS, HEAD_DIM)
    k = rope(kv[:, :, 0], positions).reshape(B, S, N_BRANCHES, N_HEADS, HEAD_DIM)
    v = kv[:, :, 1].reshape(B, S, N_BRANCHES, N_HEADS, HEAD_DIM)
    return k, v

def first_inputs(seed: int = 0) -> dict:
    key = jax.random.key(seed)
    ks = jax.random.split(key, 20)
    f32 = jnp.float32

    def w(k, shape, fan_in):
        return jax.random.normal(k, shape, f32) * (fan_in ** -0.5)

    def gain(k, shape):
        return 1.0 + 0.05 * jax.random.normal(k, shape, f32)

    x = jax.random.normal(ks[0], (BATCH, SEQ, D_MODEL), f32)
    offset = jax.random.randint(ks[1], (BATCH, 1), 0, 4096, dtype=jnp.int32)
    positions = offset + jnp.arange(SEQ, dtype=jnp.int32)[None, :]
    nA, nB = N_CONV_LAYERS, N_ATTN_LAYERS
    return {
        "x": x,
        "positions": positions,
        "mix_norm_pre": gain(ks[2], (DEPTH, D_MODEL)),
        "mix_norm_post": gain(ks[3], (DEPTH, D_MODEL)),
        "ffn_norm_pre": gain(ks[4], (DEPTH, D_MODEL)),
        "ffn_norm_post": gain(ks[5], (DEPTH, D_MODEL)),
        "ffn_w_gate_up": w(ks[6], (DEPTH, D_MODEL, 2 * D_FF), D_MODEL),
        "ffn_w_down": w(ks[7], (DEPTH, D_FF, D_MODEL), D_FF),
        "conv_w_in": w(ks[8], (nA, D_MODEL, 3 * D_MODEL), D_MODEL),
        "conv_w": w(ks[9], (nA, CONV_WIDTH, D_MODEL), CONV_WIDTH),
        "conv_w_out": w(ks[10], (nA, D_MODEL, D_MODEL), D_MODEL),
        "kv_norm": gain(ks[11], (D_MODEL,)),
        "w_kv": w(ks[12], (D_MODEL, 2 * Q_WIDTH), D_MODEL),
        "w_q": w(ks[13], (nB, D_MODEL, Q_WIDTH), D_MODEL),
        "w_o": w(ks[14], (nB, N_HEADS * HEAD_DIM, D_MODEL), N_HEADS * HEAD_DIM),
    }

def first_block(x, positions, mix_norm_pre, mix_norm_post, ffn_norm_pre, ffn_norm_post,
              ffn_w_gate_up, ffn_w_down, conv_w_in, conv_w, conv_w_out,
              kv_norm, w_kv, w_q, w_o):
    h = x
    for layer in range(DEPTH):
        if layer == N_CONV_LAYERS:
            k_sh, v_sh = shared_kv(h, positions, kv_norm, w_kv)
        hn = rms_norm(h, mix_norm_pre[layer])
        if layer < N_CONV_LAYERS:
            y = short_conv_mixer(hn, conv_w_in[layer], conv_w[layer], conv_w_out[layer])
        else:
            j = layer - N_CONV_LAYERS
            y = dilated_attention_mixer(hn, positions, k_sh, v_sh, w_q[j], w_o[j])
        h = h + rms_norm(y, mix_norm_post[layer])
        f = swiglu(rms_norm(h, ffn_norm_pre[layer]), ffn_w_gate_up[layer], ffn_w_down[layer])
        h = h + rms_norm(f, ffn_norm_post[layer])
    return h


DEPTH_2 = 1

ATTN_HEADS = 8
HEAD_DIM_2 = D_MODEL // 16
ATTN_WIDTH = ATTN_HEADS * HEAD_DIM_2
ROPE_DIM = HEAD_DIM_2 // 4
ROPE_THETA_2 = 500000.0
MOBA_BLOCK = 256
MOBA_TOP_K = 3
QUERY_CHUNK = 64
POOL_WINDOWS = (2, 4, 8, 16)
POOL_GROUPS = len(POOL_WINDOWS)
POOL_WIDTH = D_MODEL // 2
POOL_GROUP_DIM = POOL_WIDTH // POOL_GROUPS
N_BRANCHES_2 = 2
IN_WIDTH = 3 * ATTN_WIDTH + POOL_WIDTH + N_BRANCHES_2 * D_MODEL
D_FF_2 = 2816
EPS = 1e-6
NEG_INF_2 = -1e30


def rmsnorm(x, g):
    xf = x.astype(jnp.float32)
    y = xf * lax.rsqrt(jnp.mean(xf * xf, axis=-1, keepdims=True) + EPS)
    return (y * g.astype(jnp.float32)).astype(x.dtype)

def apply_partial_rotary(x, positions):
    half = ROPE_DIM // 2
    inv_freq = ROPE_THETA_2 ** (-jnp.arange(half, dtype=jnp.float32) / half)
    ang = positions.astype(jnp.float32)[:, None] * inv_freq[None, :]
    cos = jnp.cos(ang).astype(x.dtype)
    sin = jnp.sin(ang).astype(x.dtype)
    x1 = x[..., :half]
    x2 = x[..., half:ROPE_DIM]
    return jnp.concatenate([x1 * cos - x2 * sin, x2 * cos + x1 * sin, x[..., ROPE_DIM:]], axis=-1)

def moba_attention(q, k, v):
    B, H, S, Dh = q.shape
    nb = -(-S // MOBA_BLOCK)
    pad = nb * MOBA_BLOCK - S
    k_p = jnp.pad(k, ((0, 0), (0, 0), (0, pad), (0, 0)))
    v_p = jnp.pad(v, ((0, 0), (0, 0), (0, pad), (0, 0)))
    k_blk = k_p.reshape(B, H, nb, MOBA_BLOCK, Dh)
    v_blk = v_p.reshape(B, H, nb, MOBA_BLOCK, Dh)
    k_mean = jnp.mean(k_blk.astype(jnp.float32), axis=3).astype(k.dtype)
    top_k = min(MOBA_TOP_K, nb)
    scale = Dh ** -0.5
    n_chunks = S // QUERY_CHUNK
    gather_blocks = jax.vmap(jax.vmap(lambda kb, idx: kb[idx]))

    def chunk(c):
        start = c * QUERY_CHUNK
        qc = lax.dynamic_slice_in_dim(q, start, QUERY_CHUNK, axis=2)
        q_pos = start + jnp.arange(QUERY_CHUNK)
        own = start // MOBA_BLOCK
        s_blk = jnp.einsum('bhqd,bhnd->bhqn', qc, k_mean).astype(jnp.float32)
        s_blk = jnp.where(jnp.arange(nb) < own, s_blk, -jnp.inf)
        _, sel = lax.top_k(s_blk, top_k)
        sel_valid = sel < own
        k_sel = gather_blocks(k_blk, sel)
        v_sel = gather_blocks(v_blk, sel)
        logit_sel = jnp.einsum('bhqd,bhqkld->bhqkl', qc, k_sel).astype(jnp.float32) * scale
        logit_sel = jnp.where(sel_valid[..., None], logit_sel, NEG_INF_2)
        k_own = lax.dynamic_index_in_dim(k_blk, own, axis=2, keepdims=False)
        v_own = lax.dynamic_index_in_dim(v_blk, own, axis=2, keepdims=False)
        logit_own = jnp.einsum('bhqd,bhld->bhql', qc, k_own).astype(jnp.float32) * scale
        k_pos_own = own * MOBA_BLOCK + jnp.arange(MOBA_BLOCK)
        logit_own = jnp.where(k_pos_own[None, :] <= q_pos[:, None], logit_own, NEG_INF_2)
        n_sel = top_k * MOBA_BLOCK
        logits = jnp.concatenate(
            [logit_sel.reshape(B, H, QUERY_CHUNK, n_sel), logit_own], axis=-1)
        p = jax.nn.softmax(logits, axis=-1).astype(v.dtype)
        p_sel = p[..., :n_sel].reshape(B, H, QUERY_CHUNK, top_k, MOBA_BLOCK)
        p_own = p[..., n_sel:]
        return (jnp.einsum('bhqkl,bhqkld->bhqd', p_sel, v_sel)
                + jnp.einsum('bhql,bhld->bhqd', p_own, v_own))

    outs = lax.map(chunk, jnp.arange(n_chunks))
    return outs.transpose(1, 2, 0, 3, 4).reshape(B, H, S, Dh)

def multiscale_pool_mixer(u, w_pool, pool_scale):
    B, S, _ = u.shape
    ug = u.reshape(B, S, POOL_GROUPS, POOL_GROUP_DIM).astype(jnp.float32)
    cs = jnp.cumsum(ug, axis=1)
    t = jnp.arange(S, dtype=jnp.float32)[None, :, None]
    groups = []
    for g, w in enumerate(POOL_WINDOWS):
        c = cs[:, :, g]
        c_prev = jnp.pad(c, ((0, 0), (w, 0), (0, 0)))[:, :S]
        count = jnp.minimum(t + 1.0, float(w))
        groups.append((c - c_prev) / count - ug[:, :, g])
    pooled = jnp.stack(groups, axis=2).astype(u.dtype)
    mixed = jnp.einsum('bsgc,gcd->bsgd', pooled, w_pool)
    return mixed.reshape(B, S, POOL_WIDTH) * pool_scale

def causal_depthwise_conv(u, w, b):
    S = u.shape[1]
    kw = w.shape[0]
    up = jnp.pad(u, ((0, 0), (kw - 1, 0), (0, 0)))
    out = up[:, 0:S] * w[0]
    for j in range(1, kw):
        out = out + up[:, j:j + S] * w[j]
    return out + b

def hybrid_layer(x, norm_mix_g, w_in, b_gate, q_norm_g, k_norm_g, w_pool, pool_scale,
                 w_branch_attn, w_branch_pool, w_out, norm_ffn_g, w_up, conv_w, conv_b, w_down):
    B, S, D = x.shape
    h = rmsnorm(x, norm_mix_g)
    proj = h @ w_in
    q, k, v, u_pool, gate_logits = jnp.split(
        proj, [ATTN_WIDTH, 2 * ATTN_WIDTH, 3 * ATTN_WIDTH, 3 * ATTN_WIDTH + POOL_WIDTH], axis=-1)

    def heads(t):
        return t.reshape(B, S, ATTN_HEADS, HEAD_DIM_2).transpose(0, 2, 1, 3)

    pos = jnp.arange(S)
    q = apply_partial_rotary(rmsnorm(heads(q), q_norm_g), pos)
    k = apply_partial_rotary(rmsnorm(heads(k), k_norm_g), pos)
    attn = moba_attention(q, k, heads(v)).transpose(0, 2, 1, 3).reshape(B, S, ATTN_WIDTH)
    pooled = multiscale_pool_mixer(u_pool, w_pool, pool_scale)

    gates = jax.nn.sigmoid(gate_logits + b_gate).reshape(B, S, N_BRANCHES_2, D)
    mixed = gates[:, :, 0] * (attn @ w_branch_attn) + gates[:, :, 1] * (pooled @ w_branch_pool)
    x = x + mixed @ w_out

    h2 = rmsnorm(x, norm_ffn_g)
    up = causal_depthwise_conv(h2 @ w_up, conv_w, conv_b)
    gate, val = jnp.split(up, 2, axis=-1)
    return x + (jax.nn.silu(gate) * val) @ w_down

def second_inputs(seed: int = 0) -> dict:
    key = jax.random.key(seed)
    ks = jax.random.split(key, 17)
    L = DEPTH_2
    f32 = jnp.float32

    def nrm(k, shape, scale):
        return jax.random.normal(k, shape, f32) * scale

    return {
        "x": nrm(ks[0], (BATCH, SEQ, D_MODEL), 1.0),
        "norm_mix_g": 1.0 + nrm(ks[1], (L, D_MODEL), 0.02),
        "w_in": nrm(ks[2], (L, D_MODEL, IN_WIDTH), D_MODEL ** -0.5),
        "b_gate": nrm(ks[3], (L, N_BRANCHES_2 * D_MODEL), 0.1),
        "q_norm_g": 1.0 + nrm(ks[4], (L, HEAD_DIM_2), 0.02),
        "k_norm_g": 1.0 + nrm(ks[5], (L, HEAD_DIM_2), 0.02),
        "w_pool": nrm(ks[6], (L, POOL_GROUPS, POOL_GROUP_DIM, POOL_GROUP_DIM), POOL_GROUP_DIM ** -0.5),
        "pool_scale": 1.0 + nrm(ks[7], (L, POOL_WIDTH), 0.1),
        "w_branch_attn": nrm(ks[8], (L, ATTN_WIDTH, D_MODEL), ATTN_WIDTH ** -0.5),
        "w_branch_pool": nrm(ks[9], (L, POOL_WIDTH, D_MODEL), POOL_WIDTH ** -0.5),
        "w_out": nrm(ks[10], (L, D_MODEL, D_MODEL), D_MODEL ** -0.5),
        "norm_ffn_g": 1.0 + nrm(ks[11], (L, D_MODEL), 0.02),
        "w_up": nrm(ks[12], (L, D_MODEL, 2 * D_FF_2), D_MODEL ** -0.5),
        "conv_w": nrm(ks[13], (L, CONV_WIDTH, 2 * D_FF_2), CONV_WIDTH ** -0.5),
        "conv_b": nrm(ks[14], (L, 2 * D_FF_2), 0.02),
        "w_down": nrm(ks[15], (L, D_FF_2, D_MODEL), D_FF_2 ** -0.5),
    }

def second_block(x, norm_mix_g, w_in, b_gate, q_norm_g, k_norm_g, w_pool, pool_scale,
              w_branch_attn, w_branch_pool, w_out, norm_ffn_g, w_up, conv_w, conv_b, w_down):
    for l in range(DEPTH_2):
        x = hybrid_layer(x, norm_mix_g[l], w_in[l], b_gate[l], q_norm_g[l], k_norm_g[l],
                         w_pool[l], pool_scale[l], w_branch_attn[l], w_branch_pool[l], w_out[l],
                         norm_ffn_g[l], w_up[l], conv_w[l], conv_b[l], w_down[l])
    return x


def setup_inputs(seed=0):
    out = dict(first_inputs(seed))
    for name, value in second_inputs(seed + 1).items():
        if name != "x":
            out[name + "_2"] = value
    return out


def reference(
    x, positions, mix_norm_pre, mix_norm_post, ffn_norm_pre, ffn_norm_post, ffn_w_gate_up,
    ffn_w_down, conv_w_in, conv_w, conv_w_out, kv_norm, w_kv, w_q, w_o, norm_mix_g_2, w_in_2,
    b_gate_2, q_norm_g_2, k_norm_g_2, w_pool_2, pool_scale_2, w_branch_attn_2, w_branch_pool_2,
    w_out_2, norm_ffn_g_2, w_up_2, conv_w_2, conv_b_2, w_down_2,
):
    x = first_block(
        x, positions, mix_norm_pre, mix_norm_post, ffn_norm_pre, ffn_norm_post, ffn_w_gate_up,
        ffn_w_down, conv_w_in, conv_w, conv_w_out, kv_norm, w_kv, w_q, w_o,
    )
    return second_block(
        x, norm_mix_g_2, w_in_2, b_gate_2, q_norm_g_2, k_norm_g_2, w_pool_2, pool_scale_2,
        w_branch_attn_2, w_branch_pool_2, w_out_2, norm_ffn_g_2, w_up_2, conv_w_2, conv_b_2,
        w_down_2,
    )


_drawn_inputs = setup_inputs


def setup_inputs(seed=0):
    import zlib

    import numpy as np

    out = dict(_drawn_inputs(seed))
    spreads = {}
    factors = {'norm_mix_g_2': 8.0,
     'b_gate_2': 6.418,
     'q_norm_g_2': 8.0,
     'k_norm_g_2': 8.0,
     'pool_scale_2': 2.897,
     'norm_ffn_g_2': 7.173,
     'conv_b_2': 7.83}
    for name, (base, spread) in spreads.items():
        noise = np.random.default_rng([zlib.crc32(name.encode()), seed]).standard_normal(out[name].shape)
        drawn = base * np.exp(spread * noise) if base else spread * noise
        out[name] = __import__('jax').numpy.asarray(drawn.astype(out[name].dtype))
    for name, factor in factors.items():
        out[name] = (out[name] * factor).astype(out[name].dtype)
    return out
```

```python
from contextlib import ExitStack

import numpy as np

import concourse.bass as bass
from concourse import mybir

F32 = mybir.dt.float32
F32R = mybir.dt.float32r
BF16 = mybir.dt.bfloat16
I32 = mybir.dt.int32
ALU = mybir.AluOpType
ACT = mybir.ActivationFunctionType
AX = mybir.AxisListType
ds = bass.ds

P = 128
D = 1024
T = 256
KD = D // P
DFF = 2816
KF = DFF // P
HD = 64
QW = 3 * D
AW = 512
EPS = 1e-6
NEG = -1e30
QSCALE = HD ** -0.5
BRANCHES = ((128, 1), (512, 4), (2048, 16))
POOL_WINDOWS = (2, 4, 8, 16)
PI_SAFE = 3.1415925
TWO_PI_PARTS = (6.28125, 0.0019340515136718750, 1.2556659146e-6)
ROUND = 12582912.0

VECS = [[("mix_norm_pre", 16), ("mix_norm_post", 16), ("ffn_norm_pre", 16), ("ffn_norm_post", 16),
         ("kv_norm", 8), ("norm_mix_g_2", 8), ("norm_ffn_g_2", 8), ("conv_w", 24), ("pool_scale_2", 4)],
        [("conv_b_2", 44), ("conv_w_2_2", 44), ("b_gate_2", 16)],
        [("conv_w_2_01", 88)]]


class Phase:

    def __init__(self, name, count, kt, cols, pieces, loops=0, empty_last=False):
        self.name, self.count, self.kt, self.cols, self.pieces = name, count, kt, cols, pieces
        self.loops, self.empty_last = loops, empty_last

    def n(self, j, i):
        return i * 4 + (self.n0 + j)


def build(nc, a, out):
    base = (nc.sbuf_base + 31) // 32 * 32
    free = nc.sbuf_usable_end - base
    ctx = ExitStack()
    with ctx:
        ctx.enter_context(nc.sbuf_tensor("arena", [P, free // 4 - 16], F32))
        top = [base]
        names = {}

        def at(name, shape, dt, offset=None):
            size = int(np.prod(shape[1:])) * (2 if dt == BF16 else 4)
            if offset is None:
                offset = top[0]
                top[0] += (size + 31) // 32 * 32
                assert top[0] <= base + free - 64, (name, top[0] - base - free)
            names[name] = (offset, size)
            return nc.alloc_sbuf_tensor_at(name, shape, dt, offset=offset)

        def sem(name):
            return ctx.enter_context(nc.semaphore(name))

        SLOT = 3072
        raw = at("raw", [P, 2, SLOT], F32)
        w_hi = at("w_hi", [P, 4, SLOT], F32R)
        w_lo = at("w_lo", [P, 4, SLOT], F32R)
        h = at("h", [P, KD, T], F32)
        x_hi = at("x_hi", [P, KD, T], F32R)
        x_lo = at("x_lo", [P, KD, T], F32R)
        y_at = top[0]
        y = at("y", [P, KD, T], F32)
        a_at = top[0]
        a_hi = at("a_hi", [P, KF, T], F32R)
        al_at = top[0]
        a_lo = at("a_lo", [P, KF, T], F32R)
        a_end = top[0]
        mask3 = at("mask3", [P, 1152], BF16)
        m_at = names["mask3"][0]
        mask1 = at("mask1", [P, 384], BF16, m_at)
        g_qk = at("g_qk", [P, 2, HD], F32, m_at + 768)
        rope2 = at("rope2", [P, 2, 32], F32, m_at + 1280)
        rcount = at("rcount", [P, 4, 16], F32, m_at + 1536)
        ident = at("ident", [P, P], F32)
        ones = at("ones", [P, P], F32)
        cos = at("cos", [P, 2, HD], F32)
        sin = at("sin", [P, 2, HD], F32)
        vec = at("vec", [P, 308], F32)
        rstd = at("rstd", [P, T], F32)
        acc = at("acc", [P, 2, T], F32)
        sq = at("sq", [P, 2, T], F32)
        small = at("small", [P, 64], F32)
        mid = at("mid", [P, 2, 2, T], F32, y_at)
        gate = at("gate", [P, 2, 2, T], F32, y_at + 4096)
        up = at("up", [P, 2, T + 2], F32, a_at + 8192)
        cv = at("cv", [P, 2, T], F32, a_at + 8192 + 2080)
        x_tok = at("x_tok", [P, 2, D], F32, a_at)
        vec_rows = at("vec_rows", [P, 3, P], F32, a_at + 8192)
        pos_i = at("pos_i", [P, 2], I32, a_at + 12288)
        pos_f = at("pos_f", [P, 2], F32, a_at + 12320)
        invf = at("invf", [P, HD], F32, a_at + 12352)
        ang = at("ang", [P, 2, HD], F32, a_at + 12608)
        turns = at("turns", [P, 2, HD], F32, a_at + 13120)
        wrap = at("wrap", [P, 2, HD], F32, a_at + 13632)
        e = a_at
        m_hi = at("m_hi", [P, KD, T], F32R, e)
        m_lo = at("m_lo", [P, KD, T], F32R, e + 8192)
        qT = at("qT", [P, 3, T], F32, e + 16384)
        kT = at("kT", [P, 2, 3, T], F32, e + 19456)
        v_tok = at("v_tok", [P, 2, 3 * P], F32, e + 25600)
        prob = at("prob", [P, 1152], F32, e + 28672)
        probT = at("probT", [P, 1152], F32, e + 33280)
        rope_a = at("rope_a", [P, 2, 2, 3 * P], F32, e + 37888)
        rope_b = at("rope_b", [P, 2, 3 * P], F32, names["acc"][0])
        assert e + 37888 + 6144 <= a_end and names["sq"][0] == names["acc"][0] + 2048
        gates = at("gates", [P, 16, T], F32, a_at)
        u_pad = at("u_pad", [P, 4, T + 16], F32, a_at)
        s_win = [at("s2", [P, 4, T + 16], F32, a_at + 4352), at("s4", [P, 3, T + 16], F32, a_at + 8704),
                 at("s8", [P, 2, T + 16], F32, a_at + 11968), at("s16", [P, 1, T + 16], F32, a_at + 14144)]
        b = a_at + 16384
        t_hi = at("t_hi", [P, 4, T], F32R, b)
        t_lo = at("t_lo", [P, 4, T], F32R, b + 4096)
        p_hi = at("p_hi", [P, 4, T], F32R, b + 8192)
        p_lo = at("p_lo", [P, 4, T], F32R, b + 12288)
        qT2 = at("qT2", [P, 4, T], F32, b + 16384)
        kT2 = at("kT2", [P, 2, 4, T], F32, b + 20480)
        assert b + 28672 <= a_end
        v2 = at("v2", [P, 2, 4, P], F32, y_at)
        prob2 = at("prob2", [P, 384], F32, y_at + 4096)
        probT2 = at("probT2", [P, 384], F32, y_at + 5632)
        qk = at("qk", [P, 2, 2 * P], F32, names["sq"][0])
        turn_a = at("turn_a", [P, 2, 4, 16], F32, y_at + 7168)
        turn_b = at("turn_b", [P, 2, 4, 16], F32, y_at + 7680)
        fix = at("fix", [P, 4, 16], F32, y_at + 7168)

        ps = ctx.enter_context(nc.psum_tensor("ps", [P, 8, 512], F32))
        flat = ps[:].rearrange("p b c -> p (b c)")

        def rows(w, p=P):
            return w.rearrange("(k p) c -> p k c", p=p)

        up_w = [rows(a["ffn_w_gate_up"][0]), rows(a["ffn_w_gate_up"][1]), rows(a["w_up_2"][0])]
        down_w = [rows(a["ffn_w_down"][0]), rows(a["ffn_w_down"][1]), rows(a["w_down_2"][0])]
        conv_in = rows(a["conv_w_in"][0])
        conv_out = rows(a["conv_w_out"][0])
        w_q, w_kv, w_o = rows(a["w_q"][0]), rows(a["w_kv"]), rows(a["w_o"][0])
        w_in2, w_out2 = rows(a["w_in_2"][0]), rows(a["w_out_2"][0])
        w_ba, w_bp = rows(a["w_branch_attn_2"][0]), rows(a["w_branch_pool_2"][0])

        def up_pieces(w):
            return lambda j, i: [(0, KD, 0, 256, w[:, :, ds(i * 512 + (j // 2 * 256 + j % 2 * DFF), 256)])]

        def down_pieces(w):
            return lambda j, i: [(0, KF, 0, P, w[:, :, ds(i * 512 + j * P, P)])]

        def plain(w, c0=0):
            return lambda j, i: [(0, KD, 0, 256, w[:, :, ds(i * 1024 + (c0 + j * 256), 256)])]

        def attn_pieces(j, i):
            src, c0 = ((w_q, 0), (w_kv, 0), (w_kv, QW))[j]
            return [(0, KD, g * P, P, src[:, :, ds(i * P + (c0 + g * D), P)]) for g in range(3)]

        phases = [
            Phase("conv_in", 12, KD, 256,
                  lambda j, i: plain(conv_in, (1, 2, 0)[(4 * i + j) % 3] * D + (4 * i + j) // 3 * 256)(0, 0)),
            Phase("conv_out", 4, KD, 256, plain(conv_out)),
            Phase("up0", 22, KD, 256, up_pieces(up_w[0]), loops=5),
            Phase("down0", 8, KF, P, down_pieces(down_w[0])),
            Phase("qkv", 32, KD, 384, attn_pieces, empty_last=True),
            Phase("w_o", 4, KD, 256, plain(w_o)),
            Phase("up1", 22, KD, 256, up_pieces(up_w[1]), loops=5),
            Phase("down1", 8, KF, P, down_pieces(down_w[1])),
            Phase("qkv2", 4, KD, 384, lambda j, i: [
                (0, KD, g * P, P, w_in2[:, :, g * AW + j * P:g * AW + (j + 1) * P]) for g in range(3)]),
            Phase("pool_in", 2, KD, 256, plain(w_in2, 3 * AW)),
            Phase("gates_a", 2, KD, 256, plain(w_in2, 4 * AW)),
            Phase("w_pool", 1, 4, P, lambda j, i: [(0, 4, 0, P, a["w_pool_2"][0].rearrange("g c d -> c g d"))]),
            Phase("gates_b", 6, KD, 256, plain(w_in2, 4 * AW + 512)),
            Phase("branches", 4, KD, 256, lambda j, i: [(0, 4, 0, 256, w_ba[:, :, j * 256:(j + 1) * 256]),
                                                        (4, 4, 0, 256, w_bp[:, :, j * 256:(j + 1) * 256])]),
            Phase("w_out2", 4, KD, 256, plain(w_out2)),
            Phase("up2", 22, KD, 256, up_pieces(up_w[2]), loops=5),
            Phase("down2", 8, KF, P, down_pieces(down_w[2])),
        ]
        by_name = {}
        chunk_at, landed, per_slot = [], [], [0, 0]
        for ph in phases:
            ph.n0 = len(chunk_at)
            by_name[ph.name] = ph
            for l in range(ph.count):
                real = not (ph.empty_last and l % 4 == 3)
                if real:
                    per_slot[len(chunk_at) % 2] += 16 * len(ph.pieces(l % 4, l // 4))
                landed.append(per_slot[len(chunk_at) % 2])
                chunk_at.append((ph, l) if real else None)
        TOTAL = len(chunk_at)

        raw_in = [sem(f"raw_in{s}") for s in range(2)]
        hi_ready = sem("hi_ready")
        lo_ready = sem("lo_ready")
        product_done = sem("product_done")
        emptied = [sem(f"emptied{s}") for s in range(4)]
        const_in, hybrid_in, out_stored = sem("const_in"), sem("hybrid_in"), sem("out_stored")
        v_seq = sem("v_seq")
        consts_set = sem("consts_set")
        turned_in = sem("turned_in")
        h_set = sem("h_set")
        vec_set = sem("vec_set")
        angle_set, table_set = sem("angle_set"), sem("table_set")
        squared = sem("squared")
        summed = sem("summed")
        rooted = sem("rooted")
        acc_done = sem("acc_done")
        y_scaled = sem("y_scaled")
        h_added_g = sem("h_added_g")
        h_added_v = sem("h_added_v")
        normed = sem("normed")
        norm_hi = sem("norm_hi")
        norm_split = sem("norm_split")
        gate_ready = sem("gate_ready")
        conv_base = sem("conv_base")
        mid_ready = sem("mid_ready")
        mid_hi = sem("mid_hi")
        mid_split = sem("mid_split")
        zeroed = sem("zeroed")
        roped = sem("roped")
        qk_turned = sem("qk_turned")
        qk_stored = sem("qk_stored")
        v_stored = sem("v_stored")
        scored = sem("scored")
        max_set = sem("max_set")
        exped = sem("exped")
        prob_set = sem("prob_set")
        prob_turned = sem("prob_turned")
        prob_stored = sem("prob_stored")
        head_done = sem("head_done")
        o_stored = sem("o_stored")
        o_hi, o_split = sem("o_hi"), sem("o_split")
        qk_squared, qk_summed, qk_rooted = sem("qk_squared"), sem("qk_summed"), sem("qk_rooted")
        pooled = sem("pooled")
        pool_hi, pool_split = sem("pool_hi"), sem("pool_split")
        pool2_hi = sem("pool2_hi")
        turned_out, out_set = sem("turned_out"), sem("out_set")

        block = ctx.enter_context(nc.Block())

        def slot(t, s, ph):
            return t[:, s, 0:ph.kt * ph.cols].rearrange("p (k c) -> p k c", k=ph.kt)

        def flat2(t):
            return t.rearrange("p k t -> p (k t)")

        class Chain:

            def __init__(self, eng, s):
                self.eng, self.s, self.count, self.i, self.per = eng, s, 0, None, 0

            def __call__(self, ins):
                self.count += 1
                ins.then_inc(self.s, 1)
                self.eng.wait_ge(self.s, self.count if self.i is None else self.i * self.per + self.count)

            def enter(self, i, per, first=0):
                self.i, self.per, self.start = i, per, self.count
                self.count -= first * per
                self.first = first

            def leave(self, times):
                got = self.count + self.first * self.per - self.start
                assert got == self.per, (got, self.per)
                self.count = self.start + self.per * times
                self.i = None

        col, c_ = {}, 0
        for group in VECS:
            for name, n in group:
                col[name] = c_
                c_ += n

        def v(name, k):
            return vec[:, col[name] + k:col[name] + k + 1]

        unit0 = {"conv_in": 0, "up0": 4, "up1": 15, "branches": 26, "up2": 30}
        bounds = [
            (None, [("mix_norm_pre", 0)]),
            (("mix_norm_post", 0), [("ffn_norm_pre", 0)]),
            (("ffn_norm_post", 0), [("mix_norm_pre", 8), ("kv_norm", 0)]),
            (("mix_norm_post", 8), [("ffn_norm_pre", 8)]),
            (("ffn_norm_post", 8), [("norm_mix_g_2", 0)]),
            (None, [("norm_ffn_g_2", 0)]),
        ]
        norm0, sq0, sum0, add0 = [], [], [], []
        cn = cq = cs = ca = 0
        for post, pre in bounds:
            norm0.append(cn)
            sq0.append(cq)
            sum0.append(cs)
            add0.append(ca)
            cn += KD * len(pre)
            cq += KD
            cs += 2 if post else 1
            ca += KD // 2 if post else 0
        ycount = {"conv_out": 0, "down0": 4, "w_o": 12, "down1": 16}
        after = {"conv_out": 1, "down0": 2, "w_o": 3, "down1": 4, "w_out2": 5}

        def order():
            yield None, 0
            for k, ph in enumerate(phases):
                yield ph, after.get(ph.name) if k + 1 < len(phases) else None

        def run(eng, ph, body, chain=None, per=0):
            if ph.loops:
                with eng.Fori(0, ph.loops) as i:
                    if chain:
                        chain.enter(i, per)
                    for j in range(4):
                        body(j, i)
                    if chain:
                        chain.leave(ph.loops)
            for l in range(4 * ph.loops, ph.count):
                body(l % 4, l // 4)

        used = [sum(1 for m in range(n) if m % 4 == n % 4 and not (chunk_at[m] is None or chunk_at[m][0].empty_last))
                for n in range(TOTAL)]

        def wait_emptied(eng, ph, j, i, back=0):
            n = ph.n0 + j - back
            if isinstance(i, int):
                n, i = n + 4 * i, 0
            eng.wait_ge(emptied[n % 4], i + (used[n] + 1))

        def raw_level(ph, j, i):
            n = ph.n0 + j
            if isinstance(i, int):
                return landed[n + 4 * i]
            step = landed[n + 4] - landed[n]
            return i * step + landed[n]

        def next_chunk(ph, l):
            n = ph.n0 + l
            while n < TOTAL and chunk_at[n] is None:
                n += 1
            if n >= TOTAL:
                return None
            p2, l2 = chunk_at[n]
            return p2, l2 % 4, l2 // 4

        def ahead(ph, j, i, split):
            if isinstance(i, int):
                got = next_chunk(ph, 4 * i + j + 2)
                if got:
                    split(*got)
            else:
                split(ph, (j + 2) % 4, i + (j + 2) // 4)

        N_CONST = 16 * (2 + sum(len(g) for g in VECS) + 3)
        Q_BANKS, K_BANKS, V_BANKS, S_AT, O_BANK = (0, 1), (2, 3), (4, 0), 5 * 512, 7
        TURNS = 2 * 8
        HEADS = 16

        @block.sync
        def _(sp):
            def load(ph, j, i):
                n = ph.n(j, i)
                if not isinstance(i, int) or n >= 2:
                    sp.wait_ge(lo_ready, n - 1)
                s = (ph.n0 + j) % 2
                for k0, kn, c0, cw, src in ph.pieces(j, i):
                    sp.dma_start(slot(raw, s, ph)[:, k0:k0 + kn, c0:c0 + cw], src).then_inc(raw_in[s], 16)

            sp.dma_start(x_tok[:], a["x"][0].rearrange("(t p) d -> p t d", p=P)).then_inc(const_in, 16)
            sp.dma_start(ident[:], a["c_ident"]).then_inc(const_in, 16)
            load(phases[0], 0, 0)
            load(phases[0], 1, 0)
            for g, group in enumerate(VECS):
                r = 0
                for name, n in group:
                    src = {"conv_w_2_2": a["conv_w_2"][0][2:3, :], "conv_w_2_01": a["conv_w_2"][0][0:2, :],
                           "conv_w": a["conv_w"][0]}.get(name)
                    src = a[name] if src is None else src
                    if len(src.shape) == 1:
                        src = src.rearrange("(k p) -> k p", p=P)
                    else:
                        src = src.rearrange("l (k p) -> (l k) p", p=P)
                    sp.dma_start(vec_rows[r:r + n, g, :], src).then_inc(const_in, 16)
                    r += n
            for dst, src in ((mask3, "c_mask3"), (invf, "c_invf")):
                sp.dma_start(dst[:], a[src]).then_inc(const_in, 16)
            with nc.allow_non_contiguous_dma(reason="256 positions"):
                sp.dma_start(pos_i[:], a["positions"].rearrange("o (t p) -> p (o t)", p=P)).then_inc(const_in, 16)
            for ph in phases:
                if ph.name == "up1":
                    sp.wait_ge(max_set, HEADS)
                    for dst, src in ((mask1, "c_mask1"), (rope2, "c_rope2"), (rcount, "c_rcount")):
                        sp.dma_start(dst[:], a[src]).then_inc(hybrid_in, 16)
                    for w, src in enumerate(("q_norm_g_2", "k_norm_g_2")):
                        sp.dma_start(g_qk[:, w, :], a[src].broadcast_to([P, HD])).then_inc(hybrid_in, 16)
                if ph.name == "qkv":
                    with sp.Fori(0, ph.count // 4) as i:
                        for j in range(3):
                            load(ph, j, i)
                elif ph.loops:
                    run(sp, ph, lambda j, i: load(ph, j, i))
                else:
                    for l in range(2 if ph is phases[0] else 0, ph.count):
                        load(ph, l % 4, l // 4)
            sp.wait_ge(out_set, 2)
            sp.dma_start(out[0].rearrange("(t p) d -> p t d", p=P), x_tok[:]).then_inc(out_stored, 16)
            sp.wait_ge(out_stored, 16)

        @block.tensor
        def _(pe):
            def ready(ph, j, i, bank=True):
                pe.wait_ge(lo_ready, ph.n(j, i) + 1)
                n = ph.n0 + j + (4 * i if isinstance(i, int) else 0)
                if bank and (used[n] > 0 or not isinstance(i, int)):
                    pe.wait_ge(emptied[n % 4], used[n] if isinstance(i, int) else i + used[n])

            def feature_major(ph, j, hi, lo, bank=None, kt=None, k0=0, signal=True, tile=None):
                s = (ph.n0 + j) % 4
                bank = s if bank is None else bank
                wh, wl = slot(w_hi, s, ph), slot(w_lo, s, ph)
                kt = ph.kt if kt is None else kt
                for m in range(ph.cols // P):
                    c, o = slice(m * P, (m + 1) * P), ps[:, bank, m * T:(m + 1) * T]
                    for k in range(kt):
                        if tile and m == 0:
                            tile(k)
                        nc.tensor.matmul(o, wh[:, k0 + k, c], hi[:, k, :], start=(k == 0), stop=False)
                        nc.tensor.matmul(o, wh[:, k0 + k, c], lo[:, k, :], start=False, stop=False)
                        ins = nc.tensor.matmul(o, wl[:, k0 + k, c], hi[:, k, :], start=False, stop=(k == kt - 1))
                if signal:
                    ins.then_inc(product_done, 1)

            def token_major(ph, j, t, bank, hi, lo, signal=0, tile=None):
                s = (ph.n0 + j) % 4
                wh, wl = slot(w_hi, s, ph), slot(w_lo, s, ph)
                c, o = slice(t * P, (t + 1) * P), ps[:, bank, 0:384]
                for k in range(KD):
                    if tile:
                        tile(k)
                    nc.tensor.matmul(o, hi[:, k, c], wh[:, k, :], start=(k == 0), stop=False)
                    nc.tensor.matmul(o, hi[:, k, c], wl[:, k, :], start=False, stop=False)
                    ins = nc.tensor.matmul(o, lo[:, k, c], wh[:, k, :], start=False, stop=(k == KD - 1))
                if signal:
                    ins.then_inc(product_done, signal)

            def boundary(bi):
                post, pre = bounds[bi]
                s_ = sum0[bi]
                if post:
                    prev = {1: "conv_out", 2: "down0", 3: "w_o", 4: "down1"}[bi]
                    parts = 2 if by_name[prev].cols == 256 else 1
                    pe.wait_ge(acc_done, ycount[prev] + by_name[prev].count)
                    for m in range(parts):
                        ins = nc.tensor.matmul(ps[:, 4, 0:T], ones[:], acc[:, m, :], start=(m == 0),
                                               stop=(m == parts - 1))
                    ins.then_inc(summed, 1)
                    s_ += 1
                if s_ > 0:
                    pe.wait_ge(rooted, s_)
                for k in range(KD):
                    pe.wait_ge(squared, sq0[bi] + k + 1)
                    ins = nc.tensor.matmul(ps[:, 4, 0:T], ones[:], y[:, k, :], start=(k == 0), stop=(k == KD - 1))
                ins.then_inc(summed, 1)

            pe.wait_ge(const_in, N_CONST)
            for k in range(KD):
                for t in range(2):
                    c = (k % 2 * 2 + t) * P
                    ins = nc.tensor.transpose(ps[:, k // 2, c:c + P], x_tok[:, t, k * P:(k + 1) * P], ident[:])
                ins.then_inc(turned_in, 1)
            c = 0
            for g, group in enumerate(VECS):
                n = sum(r for _, r in group)
                ins = nc.tensor.transpose(ps[:, 5, c:c + n], vec_rows[0:n, g, :], ident[0:n, 0:n])
                c += n
            ins.then_inc(turned_in, 1)
            pe.wait_ge(consts_set, 1)

            def scores(q_, k_, at_, branches):
                n = len(branches)
                for qt in range(2):
                    for b_, g in enumerate(branches):
                        w = P * (qt + 1)
                        o0 = at_ + (b_ * P if qt == 0 else n_cols(n) + b_ * 256)
                        ins = nc.tensor.matmul(flat[:, o0:o0 + w], q_[:, g, qt * P:(qt + 1) * P], k_[:, g, 0:w],
                                               start=True, stop=True)
                ins.then_inc(scored, 1)

            def n_cols(n):
                return 512 if n == 3 else P

            def turn_probs(src, at_, n):
                for kt in range(2):
                    for g in range(n):
                        for qt in range(kt, 2):
                            s0 = g * P if qt == 0 else n * P + g * 256 + kt * P
                            d0 = at_ + (g * 256 + qt * P if kt == 0 else n * 256 + g * P)
                            ins = nc.tensor.transpose(flat[:, d0:d0 + P], src[:, s0:s0 + P], ident[:])
                ins.then_inc(prob_turned, 1)

            def values(o_bank, o0, hh, n, v_of, pT):
                r = slice(hh * HD, (hh + 1) * HD)
                for g in range(n):
                    nc.tensor.matmul(ps[r, o_bank, o0:o0 + T], v_of(0, g), pT[:, g * 256:(g + 1) * 256],
                                     start=(g == 0), stop=False, skip_group_check=True)
                    ins = nc.tensor.matmul(ps[r, o_bank, o0 + P:o0 + T], v_of(1, g),
                                           pT[:, n * 256 + g * P:n * 256 + (g + 1) * P], start=False,
                                           stop=(g == n - 1), skip_group_check=True)
                ins.then_inc(head_done, 1)

            def attn_step(i, project, attend):
                ph, q = by_name["qkv"], i - 1
                first = isinstance(i, int) and i == 0
                tail = isinstance(i, int) and i == 8

                def score(hh):
                    if hh == 0:
                        if not isinstance(i, int) or i > 1:
                            pe.wait_ge(prob_stored, q * 2)
                            pe.wait_ge(o_stored, q)
                        pe.wait_ge(qk_stored, q * 2 + 2)
                    scores(qT, kT[:, hh], S_AT, range(3))

                def turn_p(hh):
                    pe.wait_ge(prob_set, q * 2 + (hh + 1))
                    turn_probs(prob, S_AT, 3)

                def value(hh):
                    pe.wait_ge(prob_stored, q * 2 + (hh + 1))
                    if hh == 0:
                        pe.wait_ge(v_stored, q + 1)
                    values(O_BANK, 256, hh, 3, lambda kt, g: v_tok[:, kt, g * P + hh * HD:g * P + (hh + 1) * HD],
                           probT)

                def turn(which, banks):
                    pe.wait_ge(roped, i * 2 + (which + 1))
                    for t in range(2):
                        for g in range(3):
                            ins = nc.tensor.transpose(ps[:, banks[t], g * P:(g + 1) * P],
                                                      rope_a[:, which, t, g * P:(g + 1) * P], ident[:])
                    ins.then_inc(qk_turned, 1)

                if project:
                    ready(ph, 0, i, bank=False)
                    if not first:
                        pe.wait_ge(qk_stored, i * 2)
                    tile = (lambda k: pe.wait_ge(norm_split, norm0[2] + k + 1)) if first else None
                    token_major(ph, 0, 1, Q_BANKS[1], m_hi, m_lo, tile=tile)
                if attend:
                    score(0)
                if project:
                    if not first:
                        pe.wait_ge(v_stored, i)
                    token_major(ph, 0, 0, Q_BANKS[0], m_hi, m_lo, signal=1)
                    ready(ph, 1, i, bank=False)
                    tile = (lambda k: pe.wait_ge(norm_split, norm0[2] + KD + k + 1)) if first else None
                    token_major(ph, 1, 0, K_BANKS[0], x_hi, x_lo, tile=tile)
                if attend:
                    turn_p(0)
                if project:
                    token_major(ph, 1, 1, K_BANKS[1], x_hi, x_lo, signal=1)
                if attend:
                    value(0)
                    score(1)
                if project:
                    turn(0, Q_BANKS)
                    ready(ph, 2, i, bank=False)
                    token_major(ph, 2, 0, V_BANKS[0], x_hi, x_lo)
                    turn(1, K_BANKS)
                if attend:
                    turn_p(1)
                if project:
                    pe.wait_ge(qk_stored, i * 2 + 1)
                    token_major(ph, 2, 1, V_BANKS[1], x_hi, x_lo, signal=2)
                if attend:
                    value(1)

            def hybrid_turn(r):
                ph = by_name["qkv2"]
                bk = (ph.n0 + r) % 4
                pe.wait_ge(roped, TURNS + r + 1)
                for t in range(2):
                    for w in range(2):
                        ins = nc.tensor.transpose(ps[:, bk + 4 * t, w * P:(w + 1) * P], qk[:, t, w * P:(w + 1) * P],
                                                  ident[:])
                ins.then_inc(qk_turned, 1)

            def hybrid_head(hd, part):
                r, hh, c0 = hd // 2, hd % 2, HEADS + hd
                if part == "scores":
                    if hd > 0:
                        pe.wait_ge(max_set, c0)
                    scores(qT2, kT2[:, hh], 4 * 512, [r])
                elif part == "turn":
                    pe.wait_ge(prob_set, c0 + 1)
                    turn_probs(prob2, 5 * 512, 1)
                else:
                    pe.wait_ge(prob_stored, c0 + 1)
                    if hh == 0 and r > 0:
                        pe.wait_ge(o_split, 8 + r)
                    values(6, 0, hh, 1, lambda kt, g: v2[:, kt, r, hh * HD:(hh + 1) * HD], probT2)

            def tiles_of(count, per):
                return lambda k: pe.wait_ge(mid_split, count + k // per + 1)

            def emit(ph):
                name = ph.name
                if name == "conv_in":
                    for l in range(ph.count):
                        ready(ph, l % 4, l // 4)
                        feature_major(ph, l % 4, x_hi, x_lo,
                                      tile=(lambda k: pe.wait_ge(norm_split, k + 1)) if l == 0 else None)
                elif name in ("up0", "up1", "up2"):
                    n_ = norm0[{"up0": 1, "up1": 3, "up2": 5}[name]]
                    pe.wait_ge(norm_split, n_ + KD)

                    def body(j, i):
                        ready(ph, j, i)
                        feature_major(ph, j, x_hi, x_lo)
                    run(pe, ph, body)
                elif name in ("pool_in", "gates_a"):
                    for j in range(ph.count):
                        ready(ph, j, 0)
                        feature_major(ph, j, x_hi, x_lo)
                elif name in ("conv_out", "w_out2"):
                    hi, lo, u = (a_hi, a_lo, 0) if name == "conv_out" else (x_hi, x_lo, unit0["branches"])
                    for j in range(4):
                        ready(ph, j, 0)
                        feature_major(ph, j, hi, lo, tile=tiles_of(u, 2) if j == 0 else None)
                elif name in ("down0", "down1", "down2"):
                    u = unit0["up" + name[-1]]
                    with pe.Fori(0, 2) as i:
                        for j in range(4):
                            ready(ph, j, i)
                            feature_major(ph, j, a_hi, a_lo, tile=tiles_of(u, 2) if j == 0 else None)
                elif name == "qkv":
                    attn_step(0, True, False)
                    attn_step(1, True, True)
                    with pe.Fori(2, 8) as i:
                        attn_step(i, True, True)
                    attn_step(8, False, True)
                elif name == "w_o":
                    for j in range(4):
                        ready(ph, j, 0)
                        feature_major(ph, j, x_hi, x_lo,
                                      tile=(lambda k: pe.wait_ge(o_split, k + 1)) if j == 0 else None)
                elif name == "qkv2":
                    for r in range(4):
                        ready(ph, r, 0)
                        for t in range(2):
                            tile = (lambda k: pe.wait_ge(norm_split, norm0[4] + k + 1)) if r + t == 0 else None
                            token_major(ph, r, t, (ph.n0 + r) % 4 + 4 * t, x_hi, x_lo, signal=t, tile=tile)
                        if r > 0:
                            hybrid_turn(r - 1)
                    hybrid_turn(3)
                elif name == "w_pool":
                    ready(ph, 0, 0)
                    for r in range(4):
                        wait_emptied(pe, by_name["qkv2"], r, 0)
                    pe.wait_ge(pool_split, 1)
                    s = ph.n0 % 4
                    wh, wl = slot(w_hi, s, ph), slot(w_lo, s, ph)
                    for g in range(4):
                        o = ps[:, s if g < 2 else 7, g % 2 * T:(g % 2 + 1) * T]
                        nc.tensor.matmul(o, wh[:, g, :], t_hi[:, g, :], start=True, stop=False)
                        nc.tensor.matmul(o, wh[:, g, :], t_lo[:, g, :], start=False, stop=False)
                        ins = nc.tensor.matmul(o, wl[:, g, :], t_hi[:, g, :], start=False, stop=True)
                    ins.then_inc(product_done, 1)
                elif name == "gates_b":
                    for l in range(ph.count):
                        ready(ph, l % 4, l // 4)
                        feature_major(ph, l % 4, x_hi, x_lo)
                        if l > 0:
                            hybrid_head(l - 1, "turn")
                            hybrid_head(l - 1, "values")
                        hybrid_head(l, "scores")
                    for hd in (5, 6, 7):
                        hybrid_head(hd, "turn")
                        hybrid_head(hd, "values")
                        if hd < 7:
                            hybrid_head(hd + 1, "scores")
                elif name == "branches":
                    wait_emptied(pe, by_name["w_pool"], 0, 0)
                    pe.wait_ge(o_split, 8 + 4)
                    for j in range(4):
                        ready(ph, j, 0)
                        feature_major(ph, j, t_hi, t_lo, kt=4, signal=False)
                        feature_major(ph, j, p_hi, p_lo, bank=4 + (ph.n0 + j) % 4, kt=4, k0=4)

            for ph, bi in order():
                if ph is not None:
                    emit(ph)
                if bi is not None:
                    boundary(bi)

            last = phases[-1]
            for t in range(2):
                for k in range(KD):
                    if t == 0 and last.name == "down2":
                        wait_emptied(pe, last, k % 4, k // 4)
                    ins = nc.tensor.transpose(ps[:, 4 + 2 * t + k // 4, k % 4 * P:(k % 4 + 1) * P],
                                              h[:, k, t * P:(t + 1) * P], ident[:])
                ins.then_inc(turned_out, 1)

        @block.scalar
        def _(act):
            def split(ph, j, i):
                n, s, r = ph.n(j, i), (ph.n0 + j) % 4, (ph.n0 + j) % 2
                act.wait_ge(raw_in[r], raw_level(ph, j, i))
                if not isinstance(i, int) or n >= 4:
                    act.wait_ge(product_done, n - 3)
                size = ph.kt * ph.cols
                nc.scalar.activation(w_hi[:, s, 0:size], raw[:, r, 0:size], ACT.Copy)\
                    .then_inc(hi_ready, 2 if ph.empty_last and j == 2 else 1)

            def root(k):
                act.wait_ge(summed, k + 1)
                nc.scalar.activation(rstd[:], ps[:, 4, 0:T], ACT.Sqrt, bias=small[:, 0:1], scale=1.0 / D)\
                    .then_inc(rooted, 1)

            def boundary(bi):
                post, pre = bounds[bi]
                s_ = sum0[bi]
                if post:
                    root(s_)
                    s_ += 1
                for k in range(KD):
                    if bi == 0:
                        act.wait_ge(h_set, k // 2 + 1)
                    elif post:
                        act.wait_ge(h_added_g if k < 4 else h_added_v, add0[bi] + k % 4 + 1)
                    else:
                        wait_emptied(act, by_name["w_out2"], k // 2, 0)
                    nc.scalar.activation(y[:, k, :], h[:, k, :], ACT.Square).then_inc(squared, 1)
                root(s_)
                for r in range(len(pre)):
                    dst = m_hi if len(pre) == 2 and r == 0 else x_hi
                    for k in range(KD):
                        act.wait_ge(normed, norm0[bi] + r * KD + k + 1)
                        nc.scalar.activation(dst[:, k, :], y[:, k, :], ACT.Copy).then_inc(norm_hi, 1)

            def collect(ph, j, i):
                s, c = (ph.n0 + j) % 4, ycount[ph.name] + 4 * i + j
                act.wait_ge(product_done, ph.n(j, i) + 1)
                if ph.cols == P:
                    src, dst, sqd = ps[:, s, 0:T], y[:, 4 * i + j, :], sq[:, 0, :]
                else:
                    src, dst, sqd = ps[:, s, :], flat2(y[:, 2 * j:2 * j + 2, :]), flat2(sq[:])
                nc.scalar.activation(dst, src, ACT.Copy)
                if c > 0:
                    act.wait_ge(acc_done, c)
                nc.scalar.activation(sqd, src, ACT.Square).then_inc(emptied[s], 1)

            for k2 in range(4):
                act.wait_ge(turned_in, 2 * k2 + 2)
                nc.scalar.activation(flat2(h[:, 2 * k2:2 * k2 + 2, :]), ps[:, k2, :], ACT.Copy).then_inc(h_set, 1)
            for l in range(2):
                split(*next_chunk(phases[0], l))
            act.wait_ge(consts_set, 2)
            boundary(0)
            act.wait_ge(angle_set, 1)
            nc.scalar.activation(sin[:], turns[:], ACT.Sin).then_inc(table_set, 1)
            nc.scalar.activation(cos[:], ang[:], ACT.Sin).then_inc(table_set, 1)

            def up_body(ph):
                def body(j, i):
                    ahead(ph, j, i, split)
                    s, half = (ph.n0 + j) % 4, j // 2
                    if j % 2 == 0:
                        act.wait_ge(product_done, ph.n(j, i) + 1)
                        wait_emptied(act, ph, j, i, back=3)
                        nc.scalar.activation(flat2(gate[:, half]), ps[:, s, :], ACT.Silu).then_inc(emptied[s], 1)
                    else:
                        wait_emptied(act, ph, j, i)
                        nc.scalar.activation(a_hi[:, ds(i * 4 + half * 2, 2), :], mid[:, half], ACT.Copy)\
                            .then_inc(mid_hi, 1)
                return body

            def up_conv_body(ph):
                u0 = unit0[ph.name]

                def body(j, i):
                    ahead(ph, j, i, split)
                    s, half = (ph.n0 + j) % 4, j // 2
                    u = i * 2 + (u0 + half)
                    act.wait_ge(product_done, ph.n(j, i) + 1)
                    if j % 2 == 0:
                        act.wait_ge(mid_ready, u - 26)
                    for m in range(2):
                        f = i * 4 + (half * 2 + j % 2 * KF + m)
                        ins = nc.scalar.activation(gate[:, j % 2, m, :], ps[:, s, m * T:(m + 1) * T], ACT.Identity,
                                                   bias=vec[:, ds(f + col["conv_b_2"], 1)],
                                                   scale=vec[:, ds(f + col["conv_w_2_2"], 1)])
                    ins.then_inc(conv_base, 1)
                    if j % 2 == 1:
                        wait_emptied(act, ph, j, i, back=1)
                        nc.scalar.activation(flat2(gate[:, 0]), flat2(gate[:, 0]), ACT.Silu).then_inc(gate_ready, 1)
                        act.wait_ge(mid_ready, u - 25)
                        nc.scalar.activation(a_hi[:, ds(i * 4 + half * 2, 2), :], mid[:, half], ACT.Copy)\
                            .then_inc(mid_hi, 1)
                return body

            def softmax_exp(src, spans, c):
                act.wait_ge(max_set, c + 1)
                for t, cols in enumerate(spans):
                    nc.scalar.activation(src[:, cols], src[:, cols], ACT.Exp, bias=small[:, 4 + t:5 + t],
                                         scale=QSCALE, accum_out=small[:, 6 + t:7 + t]).then_inc(exped, 1)

            def attn_step(i, project, attend, last=False):
                ph, q = by_name["qkv"], i - 1

                def turned(hh):
                    act.wait_ge(prob_turned, q * 2 + (hh + 1))
                    nc.scalar.activation(probT[:], flat[:, S_AT:S_AT + 1152], ACT.Copy).then_inc(prob_stored, 1)

                def split_next(j):
                    if last:
                        split(*next_chunk(ph, ph.count + j))
                    else:
                        split(ph, j, i + 1)

                if project:
                    split(ph, 2, i)
                if attend:
                    softmax_exp(prob, (slice(0, 384), slice(384, 1152)), q * 2)
                if project:
                    split_next(0)
                if attend:
                    turned(0)
                if project:
                    act.wait_ge(qk_turned, i * 2 + 1)
                    for t in range(2):
                        ins = nc.scalar.activation(qT[:, :, t * P:(t + 1) * P],
                                                   ps[:, Q_BANKS[t], 0:384].rearrange("p (g c) -> p g c", g=3), ACT.Copy)
                    ins.then_inc(qk_stored, 1)
                if attend:
                    softmax_exp(prob, (slice(0, 384), slice(384, 1152)), q * 2 + 1)
                if project:
                    act.wait_ge(qk_turned, i * 2 + 2)
                    if isinstance(i, int) and i == 0:
                        act.wait_ge(zeroed, 2)
                    for hh in range(2):
                        r = slice(hh * HD, (hh + 1) * HD)
                        for t in range(2):
                            ins = nc.scalar.activation(kT[r, hh, :, t * P:(t + 1) * P],
                                                       ps[r, K_BANKS[t], 0:384].rearrange("p (g c) -> p g c", g=3),
                                                       ACT.Copy)
                    ins.then_inc(qk_stored, 1)
                if attend:
                    turned(1)
                if project:
                    split_next(1)
                if attend:
                    act.wait_ge(head_done, q * 2 + 2)
                    nc.scalar.activation(y[:, ds(q, 1), :], ps[:, O_BANK:O_BANK + 1, 256:512], ACT.Copy)\
                        .then_inc(o_stored, 1)

            def hybrid_part(what, k):
                if what == "square":
                    ph = by_name["qkv2"]
                    bk = (ph.n0 + k) % 4
                    act.wait_ge(product_done, ph.n0 + k + 1)
                    if k > 0:
                        act.wait_ge(qk_summed, k)
                    for t in range(2):
                        ins = nc.scalar.activation(acc[:, t, :], ps[:, bk + 4 * t, 0:256], ACT.Square)
                    ins.then_inc(qk_squared, 1)
                elif what == "root":
                    act.wait_ge(qk_summed, k + 1)
                    nc.scalar.activation(small[:, 16:24], small[:, 8:16], ACT.Sqrt, bias=small[:, 0:1],
                                         scale=1.0 / HD).then_inc(qk_rooted, 1)
                elif what == "store":
                    ph = by_name["qkv2"]
                    bk = (ph.n0 + k) % 4
                    act.wait_ge(qk_turned, TURNS + k + 1)
                    act.wait_ge(v_stored, 8 + k + 1)
                    if k == 0:
                        act.wait_ge(zeroed, 3)
                    for t in range(2):
                        c, bank = slice(t * P, (t + 1) * P), bk + 4 * t
                        nc.scalar.activation(qT2[:, k, c], ps[:, bank, 0:P], ACT.Copy)
                        for hh in range(2):
                            r = slice(hh * HD, (hh + 1) * HD)
                            ins = nc.scalar.activation(kT2[r, hh, k, c], ps[r, bank, P:2 * P], ACT.Copy)
                    ins.then_inc(emptied[bk], 1)
                elif what == "exp":
                    softmax_exp(prob2, (slice(0, P), slice(P, 384)), HEADS + k)
                elif what == "turned":
                    act.wait_ge(prob_turned, HEADS + k + 1)
                    nc.scalar.activation(probT2[:], flat[:, 2560:2560 + 384], ACT.Copy).then_inc(prob_stored, 1)
                else:
                    act.wait_ge(head_done, HEADS + 2 * k + 2)
                    nc.scalar.activation(t_hi[:, k, :], ps[:, 6, 0:T], ACT.Copy).then_inc(o_hi, 1)

            def sigmoid(ph, l, k0):
                s = (ph.n0 + l) % 4
                act.wait_ge(product_done, ph.n0 + l + 1)
                for m in range(2):
                    ins = nc.scalar.activation(gates[:, k0 + m, :], ps[:, s, m * T:(m + 1) * T], ACT.Sigmoid,
                                               bias=v("b_gate_2", k0 + m))
                ins.then_inc(emptied[s], 1)

            def emit(ph):
                name = ph.name
                if name == "conv_in":
                    for l in range(ph.count):
                        i, r, s = l // 3, l % 3, (ph.n0 + l) % 4
                        ahead(ph, l % 4, l // 4, split)
                        if r == 0:
                            act.wait_ge(product_done, l + 1)
                            if i >= 2:
                                wait_emptied(act, ph, (l - 5) % 4, (l - 5) // 4)
                            nc.scalar.activation(flat2(gate[:, i % 2]), ps[:, s, :], ACT.Copy)\
                                .then_inc(emptied[s], 1)
                        if r == 2:
                            wait_emptied(act, ph, l % 4, l // 4)
                            nc.scalar.activation(a_hi[:, 2 * i:2 * i + 2, :], mid[:, i % 2], ACT.Copy)\
                                .then_inc(mid_hi, 1)
                elif name in ("up0", "up1"):
                    run(act, ph, up_body(ph))
                elif name == "up2":
                    run(act, ph, up_conv_body(ph))
                elif name in ycount:
                    if name == "w_o":
                        act.wait_ge(o_stored, KD)
                        act.wait_ge(product_done, ph.n0)
                        for k in range(KD):
                            nc.scalar.activation(x_hi[:, k, :], y[:, k, :], ACT.Copy).then_inc(o_hi, 1)
                        act.wait_ge(o_split, KD)
                    for l in range(ph.count):
                        ahead(ph, l % 4, l // 4, split)
                        collect(ph, l % 4, l // 4)
                elif name == "qkv":
                    attn_step(0, True, False)
                    with act.Fori(1, 7) as i:
                        attn_step(i, True, True)
                    attn_step(7, True, True, last=True)
                    attn_step(8, False, True)
                elif name == "qkv2":
                    for r in range(4):
                        ahead(ph, r, 0, split)
                        hybrid_part("square", r)
                        hybrid_part("root", r)
                        if r > 0:
                            hybrid_part("store", r - 1)
                elif name == "pool_in":
                    for l in range(2):
                        ahead(ph, l, 0, split)
                        if l == 0:
                            hybrid_part("store", 3)
                elif name == "gates_a":
                    for l in range(2):
                        ahead(ph, l, 0, split)
                        if l == 0:
                            act.wait_ge(pooled, 1)
                            nc.scalar.activation(t_hi[:], u_pad[:, :, 16:], ACT.Copy).then_inc(pool_hi, 1)
                            act.wait_ge(pool_split, 1)
                        sigmoid(ph, l, 2 * l)
                elif name == "w_pool":
                    ahead(ph, 0, 0, split)
                    act.wait_ge(product_done, ph.n0 + 1)
                    for g in range(4):
                        ins = nc.scalar.activation(
                            p_hi[:, g, :], ps[:, ph.n0 % 4 if g < 2 else 7, g % 2 * T:(g % 2 + 1) * T],
                            ACT.Identity, scale=v("pool_scale_2", g))
                    ins.then_inc(pool2_hi, 1)
                elif name == "gates_b":
                    for l in range(ph.count):
                        ahead(ph, l % 4, l // 4, split)
                        sigmoid(ph, l, 4 + 2 * l)
                        hybrid_part("exp", l)
                        hybrid_part("turned", l) if l < 5 else None
                        if l in (1, 3):
                            hybrid_part("output", l // 2)
                    for what, k in (("turned", 5), ("output", 2), ("exp", 6), ("turned", 6), ("exp", 7),
                                    ("turned", 7), ("output", 3)):
                        hybrid_part(what, k)
                elif name == "branches":
                    for j in range(4):
                        ahead(ph, j, 0, split)
                        act.wait_ge(mid_ready, j + 1)
                        nc.scalar.activation(x_hi[:, 2 * j:2 * j + 2, :], mid[:, j % 2], ACT.Copy).then_inc(mid_hi, 1)
                elif name in ("w_out2", "down2"):
                    for l in range(ph.count):
                        ahead(ph, l % 4, l // 4, split)

            for ph, bi in order():
                if ph is not None:
                    emit(ph)
                    if bi is not None:
                        boundary(bi)
            for t in range(2):
                act.wait_ge(turned_out, t + 1)
                nc.scalar.activation(x_tok[:, t, :], flat[:, (4 + 2 * t) * 512:(6 + 2 * t) * 512], ACT.Copy)\
                    .then_inc(out_set, 1)

        @block.vector
        def _(dve):
            link = Chain(dve, v_seq)

            def split(ph, j, i):
                n, s, r = ph.n(j, i), (ph.n0 + j) % 4, (ph.n0 + j) % 2
                two = ph.empty_last and j == 2
                dve.wait_ge(hi_ready, n + (2 if two else 1))
                size = ph.kt * ph.cols
                nc.vector.tensor_tensor(w_lo[:, s, 0:size], raw[:, r, 0:size], w_hi[:, s, 0:size], ALU.subtract)\
                    .then_inc(lo_ready, 2 if two else 1)

            def boundary(bi):
                post, pre = bounds[bi]
                s_ = sum0[bi]
                if post:
                    dve.wait_ge(rooted, s_ + 1)
                    link(nc.vector.reciprocal(rstd[:], rstd[:]))
                    name, c = post
                    for k in range(KD):
                        ins = nc.vector.scalar_tensor_tensor(out=y[:, k, :], in0=y[:, k, :], scalar=v(name, c + k),
                                                             in1=rstd[:], op0=ALU.mult, op1=ALU.mult)
                        if k < 4:
                            ins.then_inc(y_scaled, 1)
                        else:
                            link(ins)
                            nc.vector.tensor_tensor(h[:, k, :], h[:, k, :], y[:, k, :], ALU.add)\
                                .then_inc(h_added_v, 1)
                    s_ += 1
                dve.wait_ge(rooted, s_ + 1)
                link(nc.vector.reciprocal(rstd[:], rstd[:]))
                total = len(pre) * KD
                for e_ in range(total + 2):
                    if e_ < total:
                        r, k = e_ // KD, e_ % KD
                        name, c = pre[r]
                        if r > 0 and k == 0:
                            dve.wait_ge(norm_split, norm0[bi] + e_ - 2)
                        nc.vector.scalar_tensor_tensor(out=y[:, k, :], in0=h[:, k, :], scalar=v(name, c + k),
                                                       in1=rstd[:], op0=ALU.mult, op1=ALU.mult).then_inc(normed, 1)
                    if e_ >= 2:
                        r, k = (e_ - 2) // KD, (e_ - 2) % KD
                        hi, lo = (m_hi, m_lo) if len(pre) == 2 and r == 0 else (x_hi, x_lo)
                        dve.wait_ge(norm_hi, norm0[bi] + e_ - 1)
                        nc.vector.tensor_tensor(lo[:, k, :], y[:, k, :], hi[:, k, :], ALU.subtract)\
                            .then_inc(norm_split, 1)

            def collect(ph, j, i):
                c = 4 * i + j
                wait_emptied(dve, ph, j, i)
                dst, src = (acc[:, 0, :], sq[:, 0, :]) if ph.cols == P else (flat2(acc[:]), flat2(sq[:]))
                if c == 0:
                    nc.vector.tensor_copy(dst, src).then_inc(acc_done, 1)
                else:
                    dve.wait_ge(acc_done, ycount[ph.name] + c)
                    nc.vector.tensor_tensor(dst, dst, src, ALU.add).then_inc(acc_done, 1)

            dve.wait_ge(turned_in, KD + 1)
            n_vec = sum(n for g in VECS for _, n in g)
            nc.vector.tensor_copy(vec[:, 0:n_vec], ps[:, 5, 0:n_vec]).then_inc(vec_set, 1)
            dve.wait_ge(vec_set, 1)
            for l in range(2):
                split(*next_chunk(phases[0], l))
            dve.wait_ge(const_in, N_CONST)
            link(nc.vector.tensor_copy(pos_f[:], pos_i[:]))
            for t in range(2):
                ins = nc.vector.tensor_scalar(ang[:, t, :], invf[:], pos_f[:, t:t + 1], None, ALU.mult)
            link(ins)
            link(nc.vector.tensor_scalar(turns[:], ang[:], 1.0 / (2 * np.pi), ROUND, ALU.mult, ALU.add))
            link(nc.vector.tensor_scalar(turns[:], turns[:], ROUND, None, ALU.subtract))
            for part in TWO_PI_PARTS:
                link(nc.vector.scalar_tensor_tensor(out=ang[:], in0=turns[:], scalar=-part, in1=ang[:],
                                                    op0=ALU.mult, op1=ALU.add))
            link(nc.vector.tensor_scalar(turns[:], ang[:], PI_SAFE, -PI_SAFE, ALU.min, ALU.max))
            link(nc.vector.tensor_scalar(ang[:], ang[:], float(np.pi / 2), None, ALU.add))
            link(nc.vector.tensor_scalar(wrap[:], ang[:], float(np.pi), -2 * float(np.pi), ALU.is_gt, ALU.mult))
            link(nc.vector.tensor_tensor(ang[:], ang[:], wrap[:], ALU.add))
            nc.vector.tensor_scalar(ang[:], ang[:], PI_SAFE, -PI_SAFE, ALU.min, ALU.max).then_inc(angle_set, 1)
            boundary(0)

            def up_body(ph):
                u0 = unit0[ph.name]

                def body(j, i):
                    ahead(ph, j, i, split)
                    s, half = (ph.n0 + j) % 4, j // 2
                    if j % 2 == 1:
                        u = i * 2 + (u0 + half)
                        wait_emptied(dve, ph, j, i, back=1)
                        dve.wait_ge(product_done, ph.n(j, i) + 1)
                        dve.wait_ge(mid_split, u - 1)
                        nc.vector.tensor_tensor(flat2(mid[:, half]), ps[:, s, :], flat2(gate[:, half]), ALU.mult)\
                            .then_inc(emptied[s], 1)
                return body

            def up_conv_body(ph):
                u0 = unit0[ph.name]

                def body(j, i):
                    ahead(ph, j, i, split)
                    s, half = (ph.n0 + j) % 4, j // 2
                    u = i * 2 + (u0 + half)
                    dve.wait_ge(conv_base, (i * 4 + j) + 1)
                    for back in (1, 2):
                        for m in range(2):
                            f = i * 4 + (half * 2 + j % 2 * KF + m + (2 - back) * 2 * KF)
                            o = gate[:, j % 2, m, back:T]
                            ins = nc.vector.scalar_tensor_tensor(
                                out=o, in0=ps[:, s, m * T:m * T + T - back],
                                scalar=vec[:, ds(f + col["conv_w_2_01"], 1)], in1=o, op0=ALU.mult, op1=ALU.add)
                        if back == 1:
                            link(ins)
                    ins.then_inc(emptied[s], 1)
                    if j % 2 == 1:
                        wait_emptied(dve, ph, j, i)
                        dve.wait_ge(gate_ready, i * 2 + (half + 1))
                        dve.wait_ge(mid_split, u - 1)
                        nc.vector.tensor_tensor(flat2(mid[:, half]), flat2(gate[:, 0]), flat2(gate[:, 1]), ALU.mult)\
                            .then_inc(mid_ready, 1)
                return body

            def masked_max(src, mask, parts, c):
                dve.wait_ge(scored, c + 1)
                if not isinstance(c, int):
                    nc.vector.memset(small[:, 40:41], 0.0)
                for t, (cols, ps0) in enumerate(parts):
                    w = cols.stop - cols.start
                    ins = nc.vector.tensor_tensor_reduce(src[:, cols], flat[:, ps0:ps0 + w], mask[:, cols], 1.0,
                                                         -3.0e38, ALU.add, ALU.max, small[:, 2 + t:3 + t])
                link(ins)
                nc.vector.tensor_scalar(small[:, 4:6], small[:, 2:4], -QSCALE, None, ALU.mult).then_inc(max_set, 1)

            def normalise(src, spans, c):
                dve.wait_ge(exped, c * 2 + 2)
                link(nc.vector.reciprocal(small[:, 10:12], small[:, 6:8]))
                for t, cols in enumerate(spans):
                    ins = nc.vector.tensor_scalar(src[:, cols], src[:, cols], small[:, 10 + t:11 + t], None, ALU.mult)
                ins.then_inc(prob_set, 1)

            def rope(i, which, banks, level):
                dve.wait_ge(product_done, level)
                if not (isinstance(i, int) and i == 0 and which == 0):
                    dve.wait_ge(roped, i * 2 + which)
                x_ = ps[:, banks[0]:banks[0] + 2, 0:384].rearrange("p t (g c) -> p t g c", c=HD)
                o = rope_a[:, which].rearrange("p t (g c) -> p t g c", c=HD)
                w = rope_b[:].rearrange("p t (g c) -> p t g c", c=HD)
                half = HD // 2

                def table(t, c0, n):
                    return t[:, :, c0:c0 + n].unsqueeze(2).to_broadcast([P, 2, 6, n])
                nc.vector.tensor_tensor(o, x_, table(cos, 0, HD), ALU.mult)
                nc.vector.tensor_tensor(w[:, :, :, 0:half], x_[:, :, :, half:HD], table(sin, 0, half), ALU.mult)
                link(nc.vector.tensor_tensor(w[:, :, :, half:HD], x_[:, :, :, 0:half], table(sin, half, half), ALU.mult))
                nc.vector.tensor_tensor(rope_a[:, which], rope_a[:, which], rope_b[:], ALU.add).then_inc(roped, 1)

            def attn_step(i, project, attend, last=False):
                ph, q = by_name["qkv"], i - 1
                parts = ((slice(0, 384), S_AT), (slice(384, 1152), S_AT + 512))
                spans = (slice(0, 384), slice(384, 1152))

                def split_next(j):
                    if last:
                        split(*next_chunk(ph, ph.count + j))
                    else:
                        split(ph, j, i + 1)

                if project:
                    split(ph, 2, i)
                if attend:
                    masked_max(prob, mask3, parts, q * 2)
                    normalise(prob, spans, q * 2)
                if project:
                    rope(i, 0, Q_BANKS, ph.n(0, i) + 1)
                    split_next(0)
                    rope(i, 1, K_BANKS, ph.n(1, i) + 1)
                if attend:
                    masked_max(prob, mask3, parts, q * 2 + 1)
                    normalise(prob, spans, q * 2 + 1)
                if project:
                    split_next(1)
                    dve.wait_ge(product_done, ph.n(3, i) + 1)
                    if attend:
                        dve.wait_ge(head_done, q * 2 + 2)
                    nc.vector.tensor_copy(v_tok[:, 0, :], ps[:, V_BANKS[0], 0:384])
                    nc.vector.tensor_copy(v_tok[:, 1, :], ps[:, V_BANKS[1], 0:384]).then_inc(v_stored, 1)

            def hybrid_qkv(r):
                ph = by_name["qkv2"]
                bk = (ph.n0 + r) % 4
                dve.wait_ge(qk_squared, r + 1)
                nc.vector.tensor_reduce(small[:, 8:16], acc[:].rearrange("p t (g c) -> p (t g) c", c=HD), AX.X, ALU.add)\
                    .then_inc(qk_summed, 1)
                dve.wait_ge(qk_rooted, r + 1)
                link(nc.vector.reciprocal(small[:, 24:32], small[:, 16:24]))
                if r > 0:
                    dve.wait_ge(qk_turned, TURNS + r)
                q4 = qk[:].rearrange("p t (g c) -> p t g c", c=HD)
                inv = small[:, 24:32].rearrange("p (t g) -> p t g", t=2).unsqueeze(3).to_broadcast([P, 2, 4, HD])
                for t in range(2):
                    ins = nc.vector.tensor_copy(v2[:, t, r, :], ps[:, bk + 4 * t, 256:384])
                ins.then_inc(v_stored, 1)
                for t in range(2):
                    ins = nc.vector.tensor_tensor(q4[:, t], ps[:, bk + 4 * t, 0:256].rearrange("p (g c) -> p g c", c=HD),
                                                  inv[:, t], ALU.mult)
                link(ins)
                for t in range(2):
                    q3 = qk[:, t, :].rearrange("p (w h c) -> p w h c", w=2, h=2)
                    ins = nc.vector.tensor_tensor(q3, q3, g_qk[:].unsqueeze(2).to_broadcast([P, 2, 2, HD]), ALU.mult)
                link(ins)

                def table(c0, n):
                    return rope2[:, :, c0:c0 + n].unsqueeze(2).to_broadcast([P, 2, 4, n])
                nc.vector.tensor_tensor(turn_a[:], q4[:, :, :, 0:16], table(0, 16), ALU.mult)
                nc.vector.tensor_tensor(turn_b[:, :, :, 0:8], q4[:, :, :, 8:16], table(16, 8), ALU.mult)
                link(nc.vector.tensor_tensor(turn_b[:, :, :, 8:16], q4[:, :, :, 0:8], table(24, 8), ALU.mult))
                nc.vector.tensor_tensor(q4[:, :, :, 0:16], turn_a[:], turn_b[:], ALU.add).then_inc(roped, 1)

            def pool_windows():
                W = T + 16
                s2, s4, s8, s16 = s_win
                link(nc.vector.tensor_tensor(s2[:, :, 1:W], u_pad[:, :, 1:W], u_pad[:, :, 0:W - 1], ALU.add))
                link(nc.vector.tensor_tensor(s4[:, :, 3:W], s2[:, 1:4, 3:W], s2[:, 1:4, 1:W - 2], ALU.add))
                link(nc.vector.tensor_tensor(s8[:, :, 7:W], s4[:, 1:3, 7:W], s4[:, 1:3, 3:W - 4], ALU.add))
                link(nc.vector.tensor_tensor(s16[:, :, 15:W], s8[:, 1:2, 15:W], s8[:, 1:2, 7:W - 8], ALU.add))
                for g in range(4):
                    ins = nc.vector.tensor_tensor(fix[:, g, :], s_win[g][:, 0, 16:32], rcount[:, g, :], ALU.mult)
                link(ins)
                link(nc.vector.tensor_tensor(fix[:], fix[:], u_pad[:, :, 16:32], ALU.subtract))
                for g in range(4):
                    u_ = u_pad[:, g, 16:W]
                    ins = nc.vector.scalar_tensor_tensor(out=u_, in0=s_win[g][:, 0, 16:W], scalar=1.0 / POOL_WINDOWS[g],
                                                         in1=u_, op0=ALU.mult, op1=ALU.subtract)
                link(ins)
                nc.vector.tensor_copy(u_pad[:, :, 16:32], fix[:]).then_inc(pooled, 1)

            def head_front(hd):
                masked_max(prob2, mask1, ((slice(0, P), 4 * 512), (slice(P, 384), 4 * 512 + P)), HEADS + hd)
                normalise(prob2, (slice(0, P), slice(P, 384)), HEADS + hd)

            def head_out(r):
                dve.wait_ge(o_hi, 8 + r + 1)
                nc.vector.tensor_tensor(t_lo[:, r, :], ps[:, 6, 0:T], t_hi[:, r, :], ALU.subtract).then_inc(o_split, 1)

            def emit(ph):
                name = ph.name
                if name == "conv_in":
                    for l in range(ph.count):
                        i, r, s = l // 3, l % 3, (ph.n0 + l) % 4
                        ahead(ph, l % 4, l // 4, split)
                        if r == 1:
                            wait_emptied(dve, ph, (l - 1) % 4, (l - 1) // 4)
                            dve.wait_ge(product_done, l + 1)
                            if i == 0:
                                dve.wait_ge(zeroed, 1)
                            nc.vector.tensor_tensor(up[:, :, 2:], ps[:, s, :].rearrange("p (m t) -> p m t", m=2),
                                                    gate[:, i % 2], ALU.mult).then_inc(emptied[s], 1)
                            wait_emptied(dve, ph, l % 4, l // 4)
                            for m in range(2):
                                ins = nc.vector.tensor_scalar(cv[:, m, :], up[:, m, 2:], v("conv_w", 16 + 2 * i + m),
                                                              None, ALU.mult)
                            link(ins)
                            for tap in (1, 0):
                                for m in range(2):
                                    ins = nc.vector.scalar_tensor_tensor(
                                        out=cv[:, m, :], in0=up[:, m, tap:tap + T],
                                        scalar=v("conv_w", 8 * tap + 2 * i + m), in1=cv[:, m, :],
                                        op0=ALU.mult, op1=ALU.add)
                                link(ins)
                        if r == 2:
                            dve.wait_ge(product_done, l + 1)
                            if i >= 2:
                                dve.wait_ge(mid_split, i - 1)
                            nc.vector.tensor_tensor(flat2(mid[:, i % 2]), ps[:, s, :], flat2(cv[:]), ALU.mult)\
                                .then_inc(emptied[s], 1)
                elif name in ("up0", "up1"):
                    run(dve, ph, up_body(ph))
                elif name == "up2":
                    run(dve, ph, up_conv_body(ph), link, 4)
                elif name in ycount:
                    if name == "w_o":
                        for k in range(KD):
                            dve.wait_ge(o_hi, k + 1)
                            nc.vector.tensor_tensor(x_lo[:, k, :], y[:, k, :], x_hi[:, k, :], ALU.subtract)\
                                .then_inc(o_split, 1)
                    for l in range(ph.count):
                        ahead(ph, l % 4, l // 4, split)
                        collect(ph, l % 4, l // 4)
                elif name == "qkv":
                    dve.wait_ge(table_set, 2)
                    attn_step(0, True, False)
                    with dve.Fori(1, 7) as i:
                        link.enter(i, 6, first=1)
                        attn_step(i, True, True)
                        link.leave(6)
                    attn_step(7, True, True, last=True)
                    attn_step(8, False, True)
                elif name == "qkv2":
                    dve.wait_ge(hybrid_in, 5 * 16)
                    for r in range(4):
                        ahead(ph, r, 0, split)
                        hybrid_qkv(r)
                elif name == "pool_in":
                    for l in range(2):
                        ahead(ph, l, 0, split)
                        s = (ph.n0 + l) % 4
                        dve.wait_ge(product_done, ph.n0 + l + 1)
                        if l == 0:
                            dve.wait_ge(zeroed, 4)
                        nc.vector.tensor_copy(u_pad[:, 2 * l:2 * l + 2, 16:],
                                              ps[:, s, :].rearrange("p (m t) -> p m t", m=2)).then_inc(emptied[s], 1)
                    wait_emptied(dve, ph, 1, 0)
                    pool_windows()
                elif name == "gates_a":
                    for l in range(2):
                        if l == 0:
                            dve.wait_ge(pool_hi, 1)
                            nc.vector.tensor_tensor(t_lo[:], u_pad[:, :, 16:], t_hi[:], ALU.subtract)\
                                .then_inc(pool_split, 1)
                        ahead(ph, l, 0, split)
                elif name == "w_pool":
                    ahead(ph, 0, 0, split)
                    dve.wait_ge(pool2_hi, 1)
                    for g in range(4):
                        ins = nc.vector.scalar_tensor_tensor(
                            out=p_lo[:, g, :], in0=ps[:, ph.n0 % 4 if g < 2 else 7, g % 2 * T:(g % 2 + 1) * T],
                            scalar=v("pool_scale_2", g), in1=p_hi[:, g, :], op0=ALU.mult, op1=ALU.subtract)
                    ins.then_inc(emptied[ph.n0 % 4], 1)
                elif name == "gates_b":
                    for l in range(ph.count):
                        ahead(ph, l % 4, l // 4, split)
                        head_front(l)
                        if l in (1, 3):
                            head_out(l // 2)
                    head_out(2)
                    head_front(6)
                    head_front(7)
                    head_out(3)
                elif name == "branches":
                    for j in range(4):
                        ahead(ph, j, 0, split)
                        s = (ph.n0 + j) % 4
                        dve.wait_ge(product_done, ph.n0 + j + 1)
                        if j == 0:
                            for l in range(2, 6):
                                wait_emptied(dve, by_name["gates_b"], l % 4, l // 4)
                        if j >= 2:
                            dve.wait_ge(mid_split, unit0["branches"] + j - 1)
                        nc.vector.tensor_tensor(flat2(mid[:, j % 2]), ps[:, s, :], flat2(gates[:, 2 * j:2 * j + 2, :]),
                                                ALU.mult)
                        nc.vector.tensor_tensor(flat2(gate[:, j % 2]), ps[:, 4 + s, :],
                                                flat2(gates[:, 8 + 2 * j:10 + 2 * j, :]), ALU.mult)\
                            .then_inc(emptied[s], 1)
                        wait_emptied(dve, ph, j, 0)
                        nc.vector.tensor_tensor(flat2(mid[:, j % 2]), flat2(mid[:, j % 2]), flat2(gate[:, j % 2]),
                                                ALU.add).then_inc(mid_ready, 1)
                elif name in ("w_out2", "down2"):
                    n = ph.cols // P
                    for l in range(ph.count):
                        ahead(ph, l % 4, l // 4, split)
                        s = (ph.n0 + l) % 4
                        dve.wait_ge(product_done, ph.n0 + l + 1)
                        h_ = flat2(h[:, n * l:n * l + n, :])
                        nc.vector.tensor_tensor(h_, h_, ps[:, s, 0:n * T], ALU.add).then_inc(emptied[s], 1)

            for ph, bi in order():
                if ph is not None:
                    emit(ph)
                    if bi is not None:
                        boundary(bi)

        @block.gpsimd
        def _(pool):
            nc.gpsimd.memset(ones[:], 1.0).then_inc(consts_set, 1)
            nc.gpsimd.memset(small[:], EPS).then_inc(consts_set, 1)
            pool.wait_ge(turned_in, KD + 1)
            nc.gpsimd.memset(up[:], 0.0).then_inc(zeroed, 1)

            def hidden_low(hi, lo, u, k0, half):
                pool.wait_ge(mid_hi, u + 1)
                nc.gpsimd.tensor_tensor(lo[:, ds(k0, 2), :], mid[:, half], hi[:, ds(k0, 2), :], ALU.subtract)\
                    .then_inc(mid_split, 1)

            for ph, bi in order():
                if ph is not None:
                    name = ph.name
                    if name == "conv_in":
                        for i in range(4):
                            hidden_low(a_hi, a_lo, i, 2 * i, i % 2)
                    elif name in ("up0", "up1", "up2"):
                        with pool.Fori(0, 5) as i:
                            for half in range(2):
                                hidden_low(a_hi, a_lo, i * 2 + (unit0[name] + half), i * 4 + 2 * half, half)
                        hidden_low(a_hi, a_lo, unit0[name] + 10, 20, 0)
                    elif name == "branches":
                        for j in range(4):
                            hidden_low(x_hi, x_lo, unit0[name] + j, 2 * j, j % 2)
                    elif name == "qkv":
                        pool.wait_ge(product_done, ph.n0)
                        nc.gpsimd.memset(kT[:], 0.0).then_inc(zeroed, 1)
                    elif name == "qkv2":
                        pool.wait_ge(product_done, ph.n0)
                        nc.gpsimd.memset(kT2[:], 0.0).then_inc(zeroed, 1)
                        nc.gpsimd.memset(u_pad[:, :, 0:16], 0.0).then_inc(zeroed, 1)
                if bi is not None and bounds[bi][0]:
                    for k in range(4):
                        pool.wait_ge(y_scaled, add0[bi] + k + 1)
                        nc.gpsimd.tensor_tensor(h[:, k, :], h[:, k, :], y[:, k, :], ALU.add).then_inc(h_added_g, 1)


def constants():
    q, k = np.arange(T)[:, None], np.arange(T)[None, :]

    def additive(ok):
        m = np.where(ok, 0.0, NEG).astype(np.float32)
        return m[0:P, 0:P], m[P:T, 0:T]

    parts = [additive((k <= q) & (q - k <= w) & ((q - k) % d == 0)) for w, d in BRANCHES]
    mask3 = np.concatenate([p[0] for p in parts] + [p[1] for p in parts], axis=1)
    mask1 = np.concatenate(additive(k <= q), axis=1)
    half = HD // 2
    f = (np.float32(10000.0) ** (-np.arange(half, dtype=np.float32) / np.float32(half))).astype(np.float32)
    invf = np.broadcast_to(np.concatenate([-f, f]), (P, HD)).copy()
    r = HD // 8
    f2 = (np.float32(500000.0) ** (-np.arange(r, dtype=np.float32) / np.float32(r))).astype(np.float32)
    ang = (np.arange(T, dtype=np.float32)[:, None] * f2[None, :]).astype(np.float32)
    c, s = np.cos(ang), np.sin(ang)
    rope2 = np.concatenate([c, c, -s, s], axis=1).astype(np.float32).reshape(2, P, 4 * r).transpose(1, 0, 2).copy()
    t = np.arange(16)
    rc = np.stack([1.0 / np.minimum(t + 1.0, w) for w in POOL_WINDOWS]).astype(np.float32)
    bf16 = mybir.dt.np(BF16)
    return {"c_ident": np.eye(P, dtype=np.float32), "c_mask3": mask3.astype(bf16), "c_mask1": mask1.astype(bf16),
            "c_invf": invf, "c_rope2": rope2, "c_rcount": np.broadcast_to(rc, (P, 4, 16)).copy()}


_INS = ["x", "positions", "mix_norm_pre", "mix_norm_post", "ffn_norm_pre", "ffn_norm_post", "ffn_w_gate_up",
        "ffn_w_down", "conv_w_in", "conv_w", "conv_w_out", "kv_norm", "w_kv", "w_q", "w_o", "norm_mix_g_2", "w_in_2",
        "b_gate_2", "q_norm_g_2", "k_norm_g_2", "w_pool_2", "pool_scale_2", "w_branch_attn_2", "w_branch_pool_2",
        "w_out_2", "norm_ffn_g_2", "w_up_2", "conv_w_2", "conv_b_2", "w_down_2"]


def kernel(**inputs):
    import concourse.bacc as bacc
    from concourse.bass_utils import run_bass_kernel_spmd as launch

    nc = bacc.Bacc("TRN2", target_bir_lowering=False, num_devices=1)
    given = {name: np.ascontiguousarray(inputs[name]) for name in _INS}
    given.update(constants())
    arrays, args = {}, {}
    for name, value in given.items():
        arrays[f"in_{name}"] = value
        args[name] = nc.dram_tensor(f"in_{name}", value.shape, mybir.dt.from_np(value.dtype),
                                    kind="ExternalInput").ap()
    out = nc.dram_tensor("out", (1, T, D), F32, kind="ExternalOutput").ap()
    build(nc, args, out)
    r = launch(nc, [arrays], core_ids=[0])
    return r.results[0]["out"]
```

```python
from contextlib import ExitStack

import numpy as np

import concourse.bass as bass
from concourse import mybir

F32 = mybir.dt.float32
F32R = mybir.dt.float32r
BF16 = mybir.dt.bfloat16
I32 = mybir.dt.int32
ALU = mybir.AluOpType
ACT = mybir.ActivationFunctionType
AX = mybir.AxisListType
ds = bass.ds

P = 128
D = 1024
T = 256
KD = D // P
DFF = 2816
KF = DFF // P
HD = 64
QW = 3 * D
AW = 512
EPS = 1e-6
NEG = -1e30
QSCALE = HD ** -0.5
BRANCHES = ((128, 1), (512, 4), (2048, 16))
POOL_WINDOWS = (2, 4, 8, 16)
PI_SAFE = 3.1415925
TWO_PI_PARTS = (6.28125, 0.0019340515136718750, 1.2556659146e-6)
ROUND = 12582912.0

VECS = [[("mix_norm_pre", 16), ("conv_w", 24)],
        [("mix_norm_post", 16), ("ffn_norm_pre", 16), ("ffn_norm_post", 16), ("kv_norm", 8), ("norm_mix_g_2", 8),
         ("norm_ffn_g_2", 8), ("pool_scale_2", 4)],
        [("conv_b_2", 44), ("conv_w_2_2", 44), ("b_gate_2", 16)],
        [("conv_w_2_01", 88)]]


class Phase:

    def __init__(self, name, count, kt, cols, pieces, loops=0, empty_last=False):
        self.name, self.count, self.kt, self.cols, self.pieces = name, count, kt, cols, pieces
        self.loops, self.empty_last = loops, empty_last

    def n(self, j, i):
        return i * 4 + (self.n0 + j)


def build(nc, a, out):
    base = (nc.sbuf_base + 31) // 32 * 32
    free = nc.sbuf_usable_end - base
    ctx = ExitStack()
    with ctx:
        ctx.enter_context(nc.sbuf_tensor("arena", [P, free // 4 - 16], F32))
        top = [base]
        names = {}

        def at(name, shape, dt, offset=None):
            size = int(np.prod(shape[1:])) * (2 if dt == BF16 else 4)
            if offset is None:
                offset = top[0]
                top[0] += (size + 31) // 32 * 32
                assert top[0] <= base + free - 64, (name, top[0] - base - free)
            names[name] = (offset, size)
            return nc.alloc_sbuf_tensor_at(name, shape, dt, offset=offset)

        def sem(name):
            return ctx.enter_context(nc.semaphore(name))

        SLOT = 3072
        raw = at("raw", [P, 2, SLOT], F32)
        w_hi = at("w_hi", [P, 4, SLOT], F32R)
        w_lo = at("w_lo", [P, 4, SLOT], F32R)
        h = at("h", [P, KD, T], F32)
        x_hi = at("x_hi", [P, KD, T], F32R)
        x_lo = at("x_lo", [P, KD, T], F32R)
        y_at = top[0]
        y = at("y", [P, KD, T], F32)
        a_at = top[0]
        a_hi = at("a_hi", [P, KF, T], F32R)
        a_lo = at("a_lo", [P, KF, T], F32R)
        a_end = top[0]
        mask3 = at("mask3", [P, 1152], BF16)
        m_at = names["mask3"][0]
        mask1 = at("mask1", [P, 384], BF16, m_at)
        g_qk = at("g_qk", [P, 2, HD], F32, m_at + 768)
        rope2 = at("rope2", [P, 2, 32], F32, m_at + 1280)
        rcount = at("rcount", [P, 4, 16], F32, m_at + 1536)
        ident = at("ident", [P, P], F32)
        ones = at("ones", [P, P], F32)
        cos = at("cos", [P, 2, HD], F32)
        sin = at("sin", [P, 2, HD], F32)
        vec = at("vec", [P, 308], F32)
        rstd = at("rstd", [P, T], F32)
        acc = at("acc", [P, 2, T], F32)
        sq = at("sq", [P, 2, T], F32)
        small = at("small", [P, 64], F32)
        mid = at("mid", [P, 2, 2, T], F32, y_at)
        gate = at("gate", [P, 2, 2, T], F32, y_at + 4096)
        up = at("up", [P, 2, T + 2], F32, a_at + 8192)
        cv = at("cv", [P, 2, T], F32, a_at + 8192 + 2080)
        x_tok = at("x_tok", [P, 2, D], F32, a_at)
        vec_rows = at("vec_rows", [P, 4, P], F32, a_at + 8192)
        pos_i = at("pos_i", [P, 2], I32, a_at + 14336)
        pos_f = at("pos_f", [P, 2], F32, a_at + 14368)
        invf = at("invf", [P, HD], F32, a_at + 14400)
        ang = at("ang", [P, 2, HD], F32, a_at + 14656)
        turns = at("turns", [P, 2, HD], F32, a_at + 15168)
        wrap = at("wrap", [P, 2, HD], F32, a_at + 15680)
        e = a_at
        m_hi = at("m_hi", [P, KD, T], F32R, e)
        m_lo = at("m_lo", [P, KD, T], F32R, e + 8192)
        qT = at("qT", [P, 3, T], F32, e + 16384)
        kT = at("kT", [P, 2, 3, T], F32, e + 19456)
        v_tok = at("v_tok", [P, 2, 3 * P], F32, e + 25600)
        prob = at("prob", [P, 1152], F32, e + 28672)
        probT = at("probT", [P, 1152], F32, e + 33280)
        rope_a = at("rope_a", [P, 2, 2, 3 * P], F32, e + 37888)
        rope_b = at("rope_b", [P, 2, 3 * P], F32, names["acc"][0])
        assert e + 37888 + 6144 <= a_end and names["sq"][0] == names["acc"][0] + 2048
        gates = at("gates", [P, 16, T], F32, a_at)
        u_pad = at("u_pad", [P, 4, T + 16], F32, a_at)
        s_win = [at("s2", [P, 4, T + 16], F32, a_at + 4352), at("s4", [P, 3, T + 16], F32, a_at + 8704),
                 at("s8", [P, 2, T + 16], F32, a_at + 11968), at("s16", [P, 1, T + 16], F32, a_at + 14144)]
        b = a_at + 16384
        t_hi = at("t_hi", [P, 4, T], F32R, b)
        t_lo = at("t_lo", [P, 4, T], F32R, b + 4096)
        p_hi = at("p_hi", [P, 4, T], F32R, b + 8192)
        p_lo = at("p_lo", [P, 4, T], F32R, b + 12288)
        qT2 = at("qT2", [P, 4, T], F32, b + 16384)
        kT2 = at("kT2", [P, 2, 4, T], F32, b + 20480)
        mix_hi = at("mix_hi", [P, KD, T], F32R, b + 16384)
        mix_lo = [at("mix_lo0", [P, 4, T], F32R, b + 24576), at("mix_lo1", [P, 4, T], F32R, names["acc"][0])]
        scaled = at("scaled", [P, 2, 2, T], F32, names["acc"][0])
        r_sq = at("r_sq", [P, T], F32, names["sq"][0])
        assert b + 28672 <= a_end
        out_tok = at("out_tok", [P, 2, D], F32, y_at)
        v2 = at("v2", [P, 2, 4, P], F32, y_at)
        prob2 = at("prob2", [P, 384], F32, y_at + 4096)
        probT2 = at("probT2", [P, 384], F32, y_at + 5632)
        qk = at("qk", [P, 2, 2 * P], F32, names["sq"][0])
        turn_a = at("turn_a", [P, 2, 4, 16], F32, y_at + 7168)
        turn_b = at("turn_b", [P, 2, 4, 16], F32, y_at + 7680)
        fix = at("fix", [P, 4, 16], F32, a_at + 15232)

        ps = ctx.enter_context(nc.psum_tensor("ps", [P, 8, 512], F32))
        flat = ps[:].rearrange("p b c -> p (b c)")

        def rows(w, p=P):
            return w.rearrange("(k p) c -> p k c", p=p)

        up_w = [rows(a["ffn_w_gate_up"][0]), rows(a["ffn_w_gate_up"][1]), rows(a["w_up_2"][0])]
        down_w = [rows(a["ffn_w_down"][0]), rows(a["ffn_w_down"][1]), rows(a["w_down_2"][0])]
        conv_in = rows(a["conv_w_in"][0])
        conv_out = rows(a["conv_w_out"][0])
        w_q, w_kv, w_o = rows(a["w_q"][0]), rows(a["w_kv"]), rows(a["w_o"][0])
        w_in2, w_out2 = rows(a["w_in_2"][0]), rows(a["w_out_2"][0])
        w_ba, w_bp = rows(a["w_branch_attn_2"][0]), rows(a["w_branch_pool_2"][0])

        def up_pieces(w):
            return lambda j, i: [(0, KD, 0, 256, w[:, :, ds(i * 512 + (j // 2 * 256 + j % 2 * DFF), 256)])]

        def down_pieces(w):
            return lambda j, i: [(0, KF, 0, P, w[:, :, ds(i * 512 + j * P, P)])]

        def plain(w, c0=0):
            return lambda j, i: [(0, KD, 0, 256, w[:, :, ds(i * 1024 + (c0 + j * 256), 256)])]

        def attn_pieces(j, i):
            src, c0 = ((w_q, 0), (w_kv, 0), (w_kv, QW))[j]
            return [(0, KD, g * P, P, src[:, :, ds(i * P + (c0 + g * D), P)]) for g in range(3)]

        phases = [
            Phase("conv_in", 12, KD, 256,
                  lambda j, i: plain(conv_in, (1, 2, 0)[(4 * i + j) % 3] * D + (4 * i + j) // 3 * 256)(0, 0)),
            Phase("conv_out", 4, KD, 256, plain(conv_out)),
            Phase("up0", 22, KD, 256, up_pieces(up_w[0]), loops=4),
            Phase("down0", 8, KF, P, down_pieces(down_w[0])),
            Phase("qkv", 32, KD, 384, attn_pieces, empty_last=True),
            Phase("w_o", 4, KD, 256, plain(w_o)),
            Phase("up1", 22, KD, 256, up_pieces(up_w[1]), loops=4),
            Phase("down1", 8, KF, P, down_pieces(down_w[1])),
            Phase("pool_in", 2, KD, 256, plain(w_in2, 3 * AW)),
            Phase("qkv2", 4, KD, 384, lambda j, i: [
                (0, KD, g * P, P, w_in2[:, :, g * AW + j * P:g * AW + (j + 1) * P]) for g in range(3)]),
            Phase("gates_a", 2, KD, 256, plain(w_in2, 4 * AW)),
            Phase("w_pool", 1, 4, P, lambda j, i: [(0, 4, 0, P, a["w_pool_2"][0].rearrange("g c d -> c g d"))]),
            Phase("gates_b", 6, KD, 256, plain(w_in2, 4 * AW + 512)),
            Phase("branches", 4, KD, 256, lambda j, i: [(0, 4, 0, 256, w_ba[:, :, j * 256:(j + 1) * 256]),
                                                        (4, 4, 0, 256, w_bp[:, :, j * 256:(j + 1) * 256])]),
            Phase("w_out2", 4, KD, 256, plain(w_out2)),
            Phase("up2", 22, KD, 256, up_pieces(up_w[2]), loops=4),
            Phase("down2", 8, KF, P, down_pieces(down_w[2])),
        ]
        by_name = {}
        chunk_at, landed, per_slot = [], [], [0, 0]
        for ph in phases:
            ph.n0 = len(chunk_at)
            by_name[ph.name] = ph
            for l in range(ph.count):
                real = not (ph.empty_last and l % 4 == 3)
                if real:
                    per_slot[len(chunk_at) % 2] += 16 * len(ph.pieces(l % 4, l // 4))
                landed.append(per_slot[len(chunk_at) % 2])
                chunk_at.append((ph, l) if real else None)
        TOTAL = len(chunk_at)

        raw_in = [sem(f"raw_in{s}") for s in range(2)]
        hi_ready = sem("hi_ready")
        lo_ready = sem("lo_ready")
        product_done = sem("product_done")
        emptied = [sem(f"emptied{s}") for s in range(4)]
        x_in, gain_in = sem("x_in"), sem("gain_in")
        const_in, hybrid_in, out_stored = sem("const_in"), sem("hybrid_in"), sem("out_stored")
        v_seq, p_seq = sem("v_seq"), sem("p_seq")
        consts_set = sem("consts_set")
        turned_in = sem("turned_in")
        h_set = sem("h_set")
        vec_set = sem("vec_set")
        angle_set, table_set = sem("angle_set"), sem("table_set")
        squared = sem("squared")
        paired = sem("paired")
        summed = sem("summed")
        rooted = sem("rooted")
        up_set = sem("up_set")
        y_squared = sem("y_squared")
        acc_done = sem("acc_done")
        y_scaled = sem("y_scaled")
        h_added_g = sem("h_added_g")
        h_added_v = sem("h_added_v")
        norm_hi = sem("norm_hi")
        norm_split = sem("norm_split")
        col_set = sem("col_set")
        silu_done = sem("silu_done")
        gate_ready = sem("gate_ready")
        conv_base = sem("conv_base")
        taps_done = sem("taps_done")
        gates_set = sem("gates_set")
        mid_ready = sem("mid_ready")
        mid_hi = sem("mid_hi")
        mid_split = sem("mid_split")
        zeroed = sem("zeroed")
        roped = sem("roped")
        qk_turned = sem("qk_turned")
        qk_stored = sem("qk_stored")
        v_stored = sem("v_stored")
        scored = sem("scored")
        max_set = sem("max_set")
        exped = sem("exped")
        prob_set = sem("prob_set")
        prob_turned = sem("prob_turned")
        prob_stored = sem("prob_stored")
        head_done = sem("head_done")
        o_stored = sem("o_stored")
        o_hi, o_split = sem("o_hi"), sem("o_split")
        qk_squared, qk_summed, qk_rooted = sem("qk_squared"), sem("qk_summed"), sem("qk_rooted")
        pooled = sem("pooled")
        pool_hi, pool_split = sem("pool_hi"), sem("pool_split")
        pool2_hi = sem("pool2_hi")
        turned_out = sem("turned_out")
        out_set, out_set_v = sem("out_set"), sem("out_set_v")

        block = ctx.enter_context(nc.Block())

        def slot(t, s, ph):
            return t[:, s, 0:ph.kt * ph.cols].rearrange("p (k c) -> p k c", k=ph.kt)

        def flat2(t):
            return t.rearrange("p k t -> p (k t)")

        class Chain:

            def __init__(self, eng, s):
                self.eng, self.s, self.count, self.i, self.per = eng, s, 0, None, 0

            def __call__(self, ins):
                self.count += 1
                ins.then_inc(self.s, 1)
                self.eng.wait_ge(self.s, self.count if self.i is None else self.i * self.per + self.count)

            def enter(self, i, per, first=0):
                self.i, self.per, self.start = i, per, self.count
                self.count -= first * per
                self.first = first

            def leave(self, times):
                got = self.count + self.first * self.per - self.start
                assert got == self.per, (got, self.per)
                self.count = self.start + self.per * times
                self.i = None

        col, c_ = {}, 0
        for group in VECS:
            for name, n in group:
                col[name] = c_
                c_ += n

        def v(name, k):
            return vec[:, col[name] + k:col[name] + k + 1]

        unit0 = {"conv_in": 0, "up0": 4, "up1": 15, "branches": 26, "up2": 30}
        bounds = [
            (None, [("mix_norm_pre", 0)]),
            (("mix_norm_post", 0), [("ffn_norm_pre", 0)]),
            (("ffn_norm_post", 0), [("mix_norm_pre", 8), ("kv_norm", 0)]),
            (("mix_norm_post", 8), [("ffn_norm_pre", 8)]),
            (("ffn_norm_post", 8), [("norm_mix_g_2", 0)]),
            (None, [("norm_ffn_g_2", 0)]),
        ]
        norm0, sq0, sum0, add0 = [], [], [], []
        cn = cq = cs = ca = 0
        for post, pre in bounds:
            norm0.append(cn)
            sq0.append(cq)
            sum0.append(cs)
            add0.append(ca)
            cn += KD * len(pre)
            cq += KD
            cs += 2 if post else 1
            ca += 1 if post else 0
        ycount = {"conv_out": 0, "down0": 4, "w_o": 12, "down1": 16}
        after = {"conv_out": 1, "down0": 2, "w_o": 3, "down1": 4, "w_out2": 5}

        pool_tiles = (2, 4, 6)

        def wait_h(eng, bi, k):
            mine = [j for j in range(KD) if (j in pool_tiles) == (k in pool_tiles)]
            eng.wait_ge(h_added_g if k in pool_tiles else h_added_v, add0[bi] * len(mine) + mine.index(k) + 1)

        rcol = small[:, 50:52]
        SUM = 7

        def by_token(t):
            return t[:].unsqueeze(1).to_broadcast([P, 2, T])

        def order():
            yield None, 0
            for k, ph in enumerate(phases):
                yield ph, after.get(ph.name) if k + 1 < len(phases) else None

        def run(eng, ph, body, chain=None, per=0, peel=0):
            for l in range(4 * peel):
                body(l % 4, l // 4)
            if ph.loops:
                with eng.Fori(peel, ph.loops) as i:
                    if chain:
                        chain.enter(i, per, first=peel)
                    for j in range(4):
                        body(j, i)
                    if chain:
                        chain.leave(ph.loops - peel)
            for l in range(4 * ph.loops, ph.count):
                body(l % 4, l // 4)

        used = [sum(1 for m in range(n) if m % 4 == n % 4 and not (chunk_at[m] is None or chunk_at[m][0].empty_last))
                for n in range(TOTAL)]

        def wait_emptied(eng, ph, j, i, back=0):
            n = ph.n0 + j - back
            if isinstance(i, int):
                n, i = n + 4 * i, 0
            eng.wait_ge(emptied[n % 4], i + (used[n] + 1))

        def raw_level(ph, j, i):
            n = ph.n0 + j
            if isinstance(i, int):
                return landed[n + 4 * i]
            step = landed[n + 4] - landed[n]
            return i * step + landed[n]

        def next_chunk(ph, l):
            n = ph.n0 + l
            while n < TOTAL and chunk_at[n] is None:
                n += 1
            if n >= TOTAL:
                return None
            p2, l2 = chunk_at[n]
            return p2, l2 % 4, l2 // 4

        def ahead(ph, j, i, split, by):
            if isinstance(i, int):
                n = ph.n0 + 4 * i + j + by
                if n < TOTAL and chunk_at[n] is not None:
                    p2, l2 = chunk_at[n]
                    split(p2, l2 % 4, l2 // 4)
            else:
                split(ph, (j + by) % 4, i + (j + by) // 4)

        N_CONST = 16 * (sum(len(g) for g in VECS[1:]) + 3)
        Q_BANKS, K_BANKS, V_BANKS, S_AT, O_BANK = (0, 1), (2, 3), (4, 0), 5 * 512, 7
        WARM, WARM0, WARM1 = 19, 18, 12
        TURNS = 2 * 8
        HEADS = 16

        def load_vectors(eng, g, signal):
            at_row = 0
            for name, n in VECS[g]:
                src = {"conv_w_2_2": a["conv_w_2"][0][2:3, :], "conv_w_2_01": a["conv_w_2"][0][0:2, :],
                       "conv_w": a["conv_w"][0]}.get(name)
                src = a[name] if src is None else src
                if len(src.shape) == 1:
                    src = src.rearrange("(k p) -> k p", p=P)
                else:
                    src = src.rearrange("l (k p) -> (l k) p", p=P)
                eng.dma_start(vec_rows[at_row:at_row + n, g, :], src).then_inc(signal, 16)
                at_row += n

        @block.sync
        def _(sp):
            def load(ph, j, i):
                n = ph.n(j, i)
                if not isinstance(i, int) or n >= 2:
                    sp.wait_ge(lo_ready, n - 1)
                s = (ph.n0 + j) % 2
                for k0, kn, c0, cw, src in ph.pieces(j, i):
                    sp.dma_start(slot(raw, s, ph)[:, k0:k0 + kn, c0:c0 + cw], src).then_inc(raw_in[s], 16)

            sp.dma_start(ident[:], a["c_ident"]).then_inc(x_in, 16)
            for t in range(2):
                sp.dma_start(x_tok[:, t, :], a["x"][0, t * P:(t + 1) * P, :]).then_inc(x_in, 16)
            load_vectors(sp, 0, gain_in)
            load(phases[0], 0, 0)
            load(phases[0], 1, 0)
            for g in range(1, len(VECS)):
                load_vectors(sp, g, const_in)
            for dst, src in ((mask3, "c_mask3"), (invf, "c_invf")):
                sp.dma_start(dst[:], a[src]).then_inc(const_in, 16)
            with nc.allow_non_contiguous_dma(reason="256 positions"):
                sp.dma_start(pos_i[:], a["positions"].rearrange("o (t p) -> p (o t)", p=P)).then_inc(const_in, 16)
            for ph in phases:
                if ph.name == "up1":
                    sp.wait_ge(max_set, HEADS)
                    for dst, src in ((mask1, "c_mask1"), (rope2, "c_rope2"), (rcount, "c_rcount")):
                        sp.dma_start(dst[:], a[src]).then_inc(hybrid_in, 16)
                    for w, src in enumerate(("q_norm_g_2", "k_norm_g_2")):
                        sp.dma_start(g_qk[:, w, :], a[src].broadcast_to([P, HD])).then_inc(hybrid_in, 16)
                if ph.name == "qkv":
                    with sp.Fori(0, ph.count // 4) as i:
                        for j in range(3):
                            load(ph, j, i)
                elif ph.loops:
                    run(sp, ph, lambda j, i: load(ph, j, i))
                else:
                    for l in range(2 if ph is phases[0] else 0, ph.count):
                        load(ph, l % 4, l // 4)
            for c, level in ((0, 1), (512, 2)):
                sp.wait_ge(out_set, level)
                if c > 0:
                    sp.wait_ge(out_set_v, 1)
                sp.dma_start(out[0, :, c:c + 512].rearrange("(t p) d -> p t d", p=P), out_tok[:, :, c:c + 512])\
                    .then_inc(out_stored, 16)
            sp.wait_ge(out_stored, 2 * 16)

        @block.tensor
        def _(pe):
            def ready(ph, j, i, bank=True):
                pe.wait_ge(lo_ready, ph.n(j, i) + 1)
                n = ph.n0 + j + (4 * i if isinstance(i, int) else 0)
                if bank and (used[n] > 0 or not isinstance(i, int)):
                    pe.wait_ge(emptied[n % 4], used[n] if isinstance(i, int) else i + used[n])

            def feature_major(ph, j, hi, lo, bank=None, kt=None, k0=0, signal=True, tile=None):
                s = (ph.n0 + j) % 4
                bank = s if bank is None else bank
                wh, wl = slot(w_hi, s, ph), slot(w_lo, s, ph)
                kt = ph.kt if kt is None else kt
                for m in range(ph.cols // P):
                    c, o = slice(m * P, (m + 1) * P), ps[:, bank, m * T:(m + 1) * T]
                    for k in range(kt):
                        if tile and m == 0:
                            tile(k)
                        low = lo[k // 4][:, k % 4, :] if isinstance(lo, list) else lo[:, k, :]
                        nc.tensor.matmul(o, wh[:, k0 + k, c], hi[:, k, :], start=(k == 0), stop=False)
                        nc.tensor.matmul(o, wh[:, k0 + k, c], low, start=False, stop=False)
                        ins = nc.tensor.matmul(o, wl[:, k0 + k, c], hi[:, k, :], start=False, stop=(k == kt - 1))
                if signal:
                    ins.then_inc(product_done, 1)

            def feature_major_first(ph, j, hi, lo, bi):
                s = (ph.n0 + j) % 4
                wh, wl = slot(w_hi, s, ph), slot(w_lo, s, ph)
                then = norm_sum(bi)
                for k in range(KD):
                    pe.wait_ge(norm_hi, norm0[bi] + k + 1)
                    for m in range(2):
                        c, o = slice(m * P, (m + 1) * P), ps[:, s, m * T:(m + 1) * T]
                        nc.tensor.matmul(o, wh[:, k, c], hi[:, k, :], start=(k == 0 and m == 0), stop=False,
                                         skip_group_check=True)
                        nc.tensor.matmul(o, wl[:, k, c], hi[:, k, :], start=False, stop=False, skip_group_check=True)
                for k in range(KD):
                    pe.wait_ge(norm_split, norm0[bi] + k + 1)
                    for m in range(2):
                        c, o = slice(m * P, (m + 1) * P), ps[:, s, m * T:(m + 1) * T]
                        ins = nc.tensor.matmul(o, wh[:, k, c], lo[:, k, :], start=False, stop=(k == KD - 1),
                                               skip_group_check=True)
                    if k == KD - 1:
                        ins.then_inc(product_done, 1)
                    then(k)

            def token_major_first(ph, t, bank, hi, lo, bi):
                s = ph.n0 % 4
                wh, wl = slot(w_hi, s, ph), slot(w_lo, s, ph)
                c, o = slice(t * P, (t + 1) * P), ps[:, bank, 0:384]
                then = norm_sum(bi)
                for k in range(KD):
                    pe.wait_ge(norm_hi, norm0[bi] + k + 1)
                    nc.tensor.matmul(o, hi[:, k, c], wh[:, k, :], start=(k == 0), stop=False)
                    nc.tensor.matmul(o, hi[:, k, c], wl[:, k, :], start=False, stop=False)
                for k in range(KD):
                    pe.wait_ge(norm_split, norm0[bi] + k + 1)
                    nc.tensor.matmul(o, lo[:, k, c], wh[:, k, :], start=False, stop=(k == KD - 1))
                    then(k)

            def output_part(ph, j, hi, lo, tiles, tile=None):
                s = (ph.n0 + j) % 4
                wh, wl = slot(w_hi, s, ph), slot(w_lo, s, ph)
                for m in range(ph.cols // P):
                    c, o = slice(m * P, (m + 1) * P), ps[:, s, m * T:(m + 1) * T]
                    for k in tiles:
                        if tile and m == 0:
                            tile(k)
                        low = lo[k // 4][:, k % 4, :] if isinstance(lo, list) else lo[:, k, :]
                        flags = dict(stop=(k == ph.kt - 1), skip_group_check=True)
                        nc.tensor.matmul(o, wh[:, k, c], hi[:, k, :], start=(k == 0 and m == 0), **flags)
                        nc.tensor.matmul(o, wh[:, k, c], low, start=False, **flags)
                        ins = nc.tensor.matmul(o, wl[:, k, c], hi[:, k, :], start=False, **flags)
                return ins

            def token_major(ph, j, t, bank, hi, lo, signal=0, tile=None):
                s = (ph.n0 + j) % 4
                wh, wl = slot(w_hi, s, ph), slot(w_lo, s, ph)
                c, o = slice(t * P, (t + 1) * P), ps[:, bank, 0:384]
                for k in range(KD):
                    if tile:
                        tile(k)
                    nc.tensor.matmul(o, hi[:, k, c], wh[:, k, :], start=(k == 0), stop=False)
                    nc.tensor.matmul(o, hi[:, k, c], wl[:, k, :], start=False, stop=False)
                    ins = nc.tensor.matmul(o, lo[:, k, c], wh[:, k, :], start=False, stop=(k == KD - 1))
                if signal:
                    ins.then_inc(product_done, signal)

            def keep_warm(n):
                for _ in range(n):
                    nc.tensor.matmul(ps[:, 6, 0:P], ones[:], ones[:], start=True, stop=True)

            def boundary(bi):
                if bounds[bi][0]:
                    prev = {1: "conv_out", 2: "down0", 3: "w_o", 4: "down1"}[bi]
                    parts, last_ = by_name[prev].cols // P, ycount[prev] + by_name[prev].count
                    pe.wait_ge(acc_done, last_ - 1 - after[prev] + 1)
                    for m in range(parts):
                        nc.tensor.matmul(ps[:, SUM, 0:T], ones[:], acc[:, m, :], start=(m == 0), stop=False)
                    pe.wait_ge(y_squared, last_)
                    for m in range(parts):
                        ins = nc.tensor.matmul(ps[:, SUM, 0:T], ones[:], sq[:, m, :], start=False,
                                               stop=(m == parts - 1))
                    ins.then_inc(summed, 1)
                    keep_warm(WARM)

            def norm_sum(bi):
                row, column = bi != 2, bi in (2, 4)
                before = sum0[bi] + (1 if bounds[bi][0] else 0)

                def then(k):
                    if k % 2 == 0:
                        return
                    k -= 1
                    if k == 0:
                        if bi > 0:
                            pe.wait_ge(rooted, before)
                    pe.wait_ge(paired, bi * (KD // 2) + k // 2 + 1)
                    flags = dict(stop=(k == KD - 2), skip_group_check=True)
                    if row:
                        ins = nc.tensor.matmul(ps[:, SUM, 0:T], ones[:], y[:, k, :], start=(k == 0), **flags)
                    if column:
                        for t in range(2):
                            ins = nc.tensor.matmul(ps[:, SUM, T + t:T + t + 1], y[:, k, t * P:(t + 1) * P],
                                                   ones[:, 0:1], start=(k == 0 and t == 0 and not row), **flags)
                    if k == KD - 2:
                        ins.then_inc(summed, 1)
                return then

            def tile_in(bi, r=0):
                return lambda k: pe.wait_ge(norm_split, norm0[bi] + r * KD + k + 1)

            def turn_vectors(g):
                n, c = sum(r for _, r in VECS[g]), sum(r for q in VECS[:g] for _, r in q)
                return nc.tensor.transpose(ps[:, 5, c:c + n], vec_rows[0:n, g, :], ident[0:n, 0:n])

            pe.wait_ge(consts_set, 1)
            keep_warm(WARM0)
            pe.wait_ge(x_in, 3 * 16)
            pe.wait_ge(gain_in, len(VECS[0]) * 16)
            turn_vectors(0).then_inc(turned_in, 1)
            for k in range(KD):
                for t in range(2):
                    c = (k % 2 * 2 + t) * P
                    ins = nc.tensor.transpose(ps[:, k // 2, c:c + P], x_tok[:, t, k * P:(k + 1) * P], ident[:])
                ins.then_inc(turned_in, 1)
            keep_warm(WARM1)

            def scores(q_, k_, at_, branches):
                n = len(branches)
                for qt in range(2):
                    for b_, g in enumerate(branches):
                        w = P * (qt + 1)
                        o0 = at_ + (b_ * P if qt == 0 else n_cols(n) + b_ * 256)
                        ins = nc.tensor.matmul(flat[:, o0:o0 + w], q_[:, g, qt * P:(qt + 1) * P], k_[:, g, 0:w],
                                               start=True, stop=True)
                ins.then_inc(scored, 1)

            def n_cols(n):
                return 512 if n == 3 else P

            def turn_probs(src, at_, n):
                for kt in range(2):
                    for g in range(n):
                        for qt in range(kt, 2):
                            s0 = g * P if qt == 0 else n * P + g * 256 + kt * P
                            d0 = at_ + (g * 256 + qt * P if kt == 0 else n * 256 + g * P)
                            ins = nc.tensor.transpose(flat[:, d0:d0 + P], src[:, s0:s0 + P], ident[:])
                ins.then_inc(prob_turned, 1)

            def values(o_bank, o0, hh, n, v_of, pT):
                r = slice(hh * HD, (hh + 1) * HD)
                for g in range(n):
                    nc.tensor.matmul(ps[r, o_bank, o0:o0 + T], v_of(0, g), pT[:, g * 256:(g + 1) * 256],
                                     start=(g == 0), stop=False, skip_group_check=True)
                    ins = nc.tensor.matmul(ps[r, o_bank, o0 + P:o0 + T], v_of(1, g),
                                           pT[:, n * 256 + g * P:n * 256 + (g + 1) * P], start=False,
                                           stop=(g == n - 1), skip_group_check=True)
                ins.then_inc(head_done, 1)

            def attn_step(i, project, attend):
                ph, q = by_name["qkv"], i - 1
                first = isinstance(i, int) and i == 0
                tail = isinstance(i, int) and i == 8

                def output_tiles(j):
                    w = by_name["w_o"]
                    if j == 0:
                        pe.wait_ge(v_stored, 8)
                    ready(w, j, 0)
                    pe.wait_ge(o_split, 6)
                    output_part(w, j, x_hi, x_lo, range(6))

                def score(hh):
                    if hh == 0:
                        if not isinstance(i, int) or i > 1:
                            pe.wait_ge(prob_stored, q * 2)
                            pe.wait_ge(o_stored, q)
                        pe.wait_ge(qk_stored, q * 2 + 2)
                    scores(qT, kT[:, hh], S_AT, range(3))

                def turn_p(hh):
                    pe.wait_ge(prob_set, q * 2 + (hh + 1))
                    turn_probs(prob, S_AT, 3)

                def value(hh):
                    pe.wait_ge(prob_stored, q * 2 + (hh + 1))
                    if hh == 0:
                        pe.wait_ge(v_stored, q + 1)
                    values(O_BANK, 256, hh, 3, lambda kt, g: v_tok[:, kt, g * P + hh * HD:g * P + (hh + 1) * HD],
                           probT)

                def turn(which, banks):
                    pe.wait_ge(roped, i * 2 + (which + 1))
                    for t in range(2):
                        for g in range(3):
                            ins = nc.tensor.transpose(ps[:, banks[t], g * P:(g + 1) * P],
                                                      rope_a[:, which, t, g * P:(g + 1) * P], ident[:])
                    ins.then_inc(qk_turned, 1)

                if project:
                    ready(ph, 0, i, bank=False)
                    if not first:
                        pe.wait_ge(qk_stored, i * 2)
                    if first:
                        token_major_first(ph, 1, Q_BANKS[1], m_hi, m_lo, 2)
                    else:
                        token_major(ph, 0, 1, Q_BANKS[1], m_hi, m_lo)
                if attend:
                    score(0)
                if tail:
                    output_tiles(0)
                if project:
                    if not first:
                        pe.wait_ge(v_stored, i)
                    token_major(ph, 0, 0, Q_BANKS[0], m_hi, m_lo, signal=1)
                    ready(ph, 1, i, bank=False)
                    token_major(ph, 1, 0, K_BANKS[0], x_hi, x_lo, tile=tile_in(2, 1) if first else None)
                if attend:
                    turn_p(0)
                if tail:
                    output_tiles(1)
                if project:
                    token_major(ph, 1, 1, K_BANKS[1], x_hi, x_lo, signal=1)
                if attend:
                    value(0)
                    score(1)
                if tail:
                    output_tiles(2)
                if project:
                    turn(0, Q_BANKS)
                    ready(ph, 2, i, bank=False)
                    token_major(ph, 2, 0, V_BANKS[0], x_hi, x_lo)
                    turn(1, K_BANKS)
                if attend:
                    turn_p(1)
                if tail:
                    output_tiles(3)
                if project:
                    pe.wait_ge(qk_stored, i * 2 + 1)
                    token_major(ph, 2, 1, V_BANKS[1], x_hi, x_lo, signal=2)
                if attend:
                    value(1)

            def hybrid_turn(r):
                ph = by_name["qkv2"]
                bk = (ph.n0 + r) % 4
                pe.wait_ge(roped, TURNS + r + 1)
                for t in range(2):
                    for w in range(2):
                        ins = nc.tensor.transpose(ps[:, bk + 4 * t, w * P:(w + 1) * P], qk[:, t, w * P:(w + 1) * P],
                                                  ident[:])
                ins.then_inc(qk_turned, 1)

            def hybrid_head(hd, part):
                r, hh, c0 = hd // 2, hd % 2, HEADS + hd
                if part == "scores":
                    if hd > 0:
                        pe.wait_ge(max_set, c0)
                    scores(qT2, kT2[:, hh], 4 * 512, [r])
                elif part == "turn":
                    pe.wait_ge(prob_set, c0 + 1)
                    turn_probs(prob2, 5 * 512, 1)
                else:
                    pe.wait_ge(prob_stored, c0 + 1)
                    if hh == 0 and r > 0:
                        pe.wait_ge(o_split, 8 + r)
                    values(6, 0, hh, 1, lambda kt, g: v2[:, kt, r, hh * HD:(hh + 1) * HD], probT2)

            def hybrid_step(hd):
                if hd > 0:
                    hybrid_head(hd - 1, "turn")
                    hybrid_head(hd - 1, "values")
                hybrid_head(hd, "scores")

            def last_two_late(ph, hi, lo, u):
                kt, tile = ph.kt, tiles_of(u, 2)
                for j in range(2):
                    ready(ph, j, 0)
                    output_part(ph, j, hi, lo, range(kt - 2), tile=tile if j == 0 else None)
                for j in range(2):
                    output_part(ph, j, hi, lo, range(kt - 2, kt), tile=tile if j == 0 else None)\
                        .then_inc(product_done, 1)

            def turn_out(k):
                wait_emptied(pe, by_name["down2"], k % 4, k // 4)
                for t in range(2):
                    ins = nc.tensor.transpose(ps[:, 4 + 2 * t + k // 4, k % 4 * P:(k % 4 + 1) * P],
                                              h[:, k, t * P:(t + 1) * P], ident[:])
                if k % 4 == 3:
                    ins.then_inc(turned_out, 1)

            def pool_part(ph, j):
                ready(ph, j, 0)
                feature_major(ph, j, p_hi, p_lo, bank=4 + (ph.n0 + j) % 4, kt=4, k0=4, signal=False)

            def tiles_of(count, per):
                return lambda k: pe.wait_ge(mid_split, count + k // per + 1)

            def emit(ph):
                name = ph.name
                if name == "conv_in":
                    for l in range(ph.count):
                        ready(ph, l % 4, l // 4)
                        if l == 1:
                            pe.wait_ge(const_in, N_CONST)
                            for g in range(1, len(VECS)):
                                ins = turn_vectors(g)
                            ins.then_inc(turned_in, 1)
                        if l == 0:
                            feature_major_first(ph, 0, x_hi, x_lo, 0)
                        else:
                            feature_major(ph, l % 4, x_hi, x_lo)
                elif name in ("up0", "up1", "up2"):
                    bi = {"up0": 1, "up1": 3, "up2": 5}[name]

                    def body(j, i):
                        first = isinstance(i, int) and i + j == 0
                        ready(ph, j, i)
                        if first:
                            feature_major_first(ph, 0, x_hi, x_lo, bi)
                        else:
                            feature_major(ph, j, x_hi, x_lo)
                    run(pe, ph, body, peel=1)
                elif name in ("pool_in", "gates_a"):
                    for j in range(ph.count):
                        ready(ph, j, 0)
                        if name == "pool_in" and j == 0:
                            feature_major_first(ph, 0, x_hi, x_lo, 4)
                        else:
                            feature_major(ph, j, x_hi, x_lo)
                        if name == "gates_a":
                            if j == 0:
                                for r in (0, 2):
                                    wait_emptied(pe, by_name["qkv2"], r, 0)
                            else:
                                wait_emptied(pe, by_name["qkv2"], 3, 0)
                            hybrid_step(j)
                            if j == 0:
                                hybrid_turn(3)
                elif name in ("conv_out", "w_out2"):
                    hi, lo, u = (a_hi, a_lo, 0) if name == "conv_out" else (mix_hi, mix_lo, unit0["branches"])
                    last_two_late(ph, hi, lo, u)
                    for j in (2, 3):
                        ready(ph, j, 0)
                        feature_major(ph, j, hi, lo)
                elif name == "down2":
                    last_two_late(ph, a_hi, a_lo, unit0["up2"])
                    for l in range(2, ph.count):
                        ready(ph, l % 4, l // 4)
                        feature_major(ph, l % 4, a_hi, a_lo)
                        turn_out(l - 2)
                elif name in ("down0", "down1"):
                    u = unit0["up" + name[-1]]
                    with pe.Fori(0, 2) as i:
                        for j in range(4):
                            ready(ph, j, i)
                            feature_major(ph, j, a_hi, a_lo, tile=tiles_of(u, 2) if j == 0 else None)
                elif name == "qkv":
                    attn_step(0, True, False)
                    attn_step(1, True, True)
                    with pe.Fori(2, 8) as i:
                        attn_step(i, True, True)
                    attn_step(8, False, True)
                elif name == "w_o":
                    for j in range(4):
                        pe.wait_ge(o_split, 7 if j == 0 else KD)
                        if j == 0:
                            output_part(ph, 0, x_hi, x_lo, (6,))
                            output_part(ph, 1, x_hi, x_lo, (6,))
                            pe.wait_ge(o_split, KD)
                        output_part(ph, j, x_hi, x_lo, (7,) if j < 2 else (6, 7)).then_inc(product_done, 1)
                elif name == "qkv2":
                    for r in range(4):
                        ready(ph, r, 0)
                        for t in range(2):
                            if (ph.n0 + r) % 4 + 4 * t == SUM:
                                pe.wait_ge(rooted, sum0[4] + 2)
                            token_major(ph, r, t, (ph.n0 + r) % 4 + 4 * t, x_hi, x_lo, signal=t)
                        if r > 0:
                            hybrid_turn(r - 1)
                elif name == "w_pool":
                    ready(ph, 0, 0)
                    pe.wait_ge(pool_split, 1)
                    s = ph.n0 % 4
                    wh, wl = slot(w_hi, s, ph), slot(w_lo, s, ph)
                    for g in range(4):
                        o = ps[:, s if g < 2 else 7, g % 2 * T:(g % 2 + 1) * T]
                        nc.tensor.matmul(o, wh[:, g, :], t_hi[:, g, :], start=True, stop=False)
                        nc.tensor.matmul(o, wh[:, g, :], t_lo[:, g, :], start=False, stop=False)
                        ins = nc.tensor.matmul(o, wl[:, g, :], t_hi[:, g, :], start=False, stop=True)
                    ins.then_inc(product_done, 1)
                elif name == "gates_b":
                    for l in range(ph.count):
                        ready(ph, l % 4, l // 4)
                        feature_major(ph, l % 4, x_hi, x_lo)
                        hybrid_step(l + 2)
                elif name == "branches":
                    wait_emptied(pe, by_name["w_pool"], 0, 0)
                    pool_part(ph, 0)
                    hybrid_head(7, "turn")
                    pe.wait_ge(max_set, HEADS + 8)
                    pool_part(ph, 1)
                    hybrid_head(7, "values")
                    pe.wait_ge(o_split, 8 + 4)
                    for j in range(4):
                        if j > 1:
                            pool_part(ph, j)
                        feature_major(ph, j, t_hi, t_lo, kt=4)

            for ph, bi in order():
                if ph is not None:
                    emit(ph)
                if bi is not None:
                    boundary(bi)

            for k in (6, 7):
                turn_out(k)

        @block.scalar
        def _(act):
            def split(ph, j, i):
                n, s, r = ph.n(j, i), (ph.n0 + j) % 4, (ph.n0 + j) % 2
                act.wait_ge(raw_in[r], raw_level(ph, j, i))
                if not isinstance(i, int) or n >= 4:
                    act.wait_ge(product_done, n - 3)
                size = ph.kt * ph.cols
                nc.scalar.activation(w_hi[:, s, 0:size], raw[:, r, 0:size], ACT.Copy)\
                    .then_inc(hi_ready, 2 if ph.empty_last and j == 2 else 1)

            def root(k):
                act.wait_ge(summed, k + 1)
                nc.scalar.activation(rstd[:], ps[:, SUM, 0:T], ACT.Sqrt, bias=small[:, 0:1], scale=1.0 / D)\
                    .then_inc(rooted, 1)

            def high(bi, r, k, src=None):
                name, c = bounds[bi][1][r]
                dst = m_hi if bi == 2 and r == 0 else x_hi
                nc.scalar.activation(dst[:, k, :], h[:, k, :] if src is None else src, ACT.Identity,
                                     scale=v(name, c + k)).then_inc(norm_hi, 1)

            def square(k):
                nc.scalar.activation(y[:, k, :], h[:, k, :], ACT.Square).then_inc(squared, 1)

            def root_input(bi):
                act.wait_ge(summed, sum0[bi] + (2 if bounds[bi][0] else 1))
                if bi in (2, 4):
                    ins = nc.scalar.activation(small[:, 48:50], ps[:, SUM, T:T + 2], ACT.Sqrt, bias=small[:, 0:1],
                                               scale=1.0 / D)
                if bi != 2:
                    ins = nc.scalar.activation(rstd[:], ps[:, SUM, 0:T], ACT.Sqrt, bias=small[:, 0:1],
                                               scale=1.0 / D)
                ins.then_inc(rooted, 1)

            def warm(bi):
                nc.scalar.activation(small[:, 56 + bi:57 + bi], small[:, 0:1], ACT.Sqrt)

            def boundary(bi, prev):
                if bounds[bi][0]:
                    root(sum0[bi])
                    if bi == 3:
                        ahead(prev, 2, 0, split, 3)
                    for k in range(KD):
                        wait_h(act, bi, k)
                        high(bi, 0, k)
                        square(k)
                    if bi == 2:
                        for k in range(KD):
                            high(bi, 1, k)
                    ahead(prev, (prev.count - 1) % 4, (prev.count - 1) // 4, split, 3)
                root_input(bi)

            def collect(ph, j, i):
                s, c = (ph.n0 + j) % 4, ycount[ph.name] + 4 * i + j
                act.wait_ge(product_done, ph.n(j, i) + 1)
                if ph.cols == P:
                    src, dst, sqd = ps[:, s, 0:T], y[:, 4 * i + j, :], sq[:, 0, :]
                else:
                    src, dst, sqd = ps[:, s, :], flat2(y[:, 2 * j:2 * j + 2, :]), flat2(sq[:])
                if 4 * i + j > 0:
                    act.wait_ge(acc_done, c - after[ph.name] + 1)
                nc.scalar.activation(sqd, src, ACT.Square).then_inc(y_squared, 1)
                nc.scalar.activation(dst, src, ACT.Copy).then_inc(emptied[s], 1)

            act.wait_ge(consts_set, 2)
            warm(0)
            act.wait_ge(vec_set, 1)
            for k in range(KD):
                if k == 1:
                    split(*next_chunk(phases[0], 0))
                if k % 2 == 0:
                    act.wait_ge(h_set, k // 2 + 1)
                high(0, 0, k)
                square(k)
            split(*next_chunk(phases[0], 1))
            root_input(0)
            split(*next_chunk(phases[0], 2))

            def up_body(ph):
                def body(j, i):
                    half = j // 2
                    if j % 2 == 0:
                        wait_emptied(act, ph, j, i)
                        nc.scalar.activation(flat2(gate[:, half]), flat2(gate[:, half]), ACT.Silu)\
                            .then_inc(silu_done, 1)
                    else:
                        wait_emptied(act, ph, j, i)
                        nc.scalar.activation(a_hi[:, ds(i * 4 + half * 2, 2), :], mid[:, half], ACT.Copy)\
                            .then_inc(mid_hi, 1)
                    ahead(ph, j, i, split, 3)
                return body

            def last_high(ph, u):
                act.wait_ge(mid_ready, 4 + u + 1)
                nc.scalar.activation(a_hi[:, ds(u * 2, 2), :], mid[:, 0], ACT.Copy).then_inc(mid_hi, 1)

            def up_conv_body(ph):
                def body(j, i):
                    first = isinstance(i, int) and i + j == 0
                    u = i * 2 + j // 2
                    if j % 2 == 0 and not first:
                        act.wait_ge(mid_ready, 4 + u)
                    wait_emptied(act, ph, j, i)
                    for m in range(2):
                        f = i * 4 + (j // 2 * 2 + j % 2 * KF + m)
                        ins = nc.scalar.activation(gate[:, j % 2, m, :], scaled[:, j % 2, m, :], ACT.Identity,
                                                   bias=vec[:, ds(f + col["conv_b_2"], 1)],
                                                   scale=vec[:, ds(f + col["conv_w_2_2"], 1)])
                    ins.then_inc(conv_base, 1)
                    if j % 2 == 0 and not first:
                        last_high(ph, u - 1)
                    if j % 2 == 1:
                        act.wait_ge(taps_done, i * 4 + j)
                        nc.scalar.activation(flat2(gate[:, 0]), flat2(gate[:, 0]), ACT.Silu).then_inc(silu_done, 1)
                    ahead(ph, j, i, split, 3)
                return body

            def softmax_exp(src, spans, c):
                act.wait_ge(max_set, c + 1)
                for t, cols in enumerate(spans):
                    nc.scalar.activation(src[:, cols], src[:, cols], ACT.Exp, bias=small[:, 4 + t:5 + t],
                                         scale=QSCALE, accum_out=small[:, 6 + t:7 + t]).then_inc(exped, 1)

            def attn_step(i, project, attend, last=False):
                ph, q = by_name["qkv"], i - 1
                i_tail, w_o_ = not project, by_name["w_o"]

                def turned(hh):
                    act.wait_ge(prob_turned, q * 2 + (hh + 1))
                    nc.scalar.activation(probT[:], flat[:, S_AT:S_AT + 1152], ACT.Copy).then_inc(prob_stored, 1)

                def split_next(j):
                    if last:
                        split(*next_chunk(ph, ph.count + j))
                    else:
                        split(ph, j, i + 1)

                if project and attend:
                    split(ph, 2, i)
                if i_tail:
                    split(w_o_, 2, 0)
                if attend:
                    softmax_exp(prob, (slice(0, 384), slice(384, 1152)), q * 2)
                if project:
                    split_next(0)
                if attend:
                    turned(0)
                if project:
                    act.wait_ge(qk_turned, i * 2 + 1)
                    for t in range(2):
                        ins = nc.scalar.activation(qT[:, :, t * P:(t + 1) * P],
                                                   ps[:, Q_BANKS[t], 0:384].rearrange("p (g c) -> p g c", g=3), ACT.Copy)
                    ins.then_inc(qk_stored, 1)
                if attend:
                    softmax_exp(prob, (slice(0, 384), slice(384, 1152)), q * 2 + 1)
                if project:
                    act.wait_ge(qk_turned, i * 2 + 2)
                    if isinstance(i, int) and i == 0:
                        act.wait_ge(zeroed, 2)
                    for hh in range(2):
                        r = slice(hh * HD, (hh + 1) * HD)
                        for t in range(2):
                            ins = nc.scalar.activation(kT[r, hh, :, t * P:(t + 1) * P],
                                                       ps[r, K_BANKS[t], 0:384].rearrange("p (g c) -> p g c", g=3),
                                                       ACT.Copy)
                    ins.then_inc(qk_stored, 1)
                if i_tail:
                    split(w_o_, 3, 0)
                    warm(3)
                if attend:
                    turned(1)
                if project:
                    split_next(1)
                if last:
                    act.wait_ge(product_done, ph.n0 + ph.count)
                    act.wait_ge(o_stored, 6)
                    nc.scalar.activation(flat2(x_hi[:, 0:6, :]), flat2(y[:, 0:6, :]), ACT.Copy).then_inc(o_hi, 6)
                if i_tail:
                    act.wait_ge(head_done, HEADS)
                    nc.scalar.activation(x_hi[:, 7, :], ps[:, O_BANK, 256:512], ACT.Copy).then_inc(o_hi, 1)
                elif attend:
                    act.wait_ge(head_done, q * 2 + 2)
                    nc.scalar.activation(y[:, ds(q, 1), :], ps[:, O_BANK:O_BANK + 1, 256:512], ACT.Copy)\
                        .then_inc(o_stored, 1)
                if last:
                    act.wait_ge(o_stored, 7)
                    nc.scalar.activation(x_hi[:, 6, :], y[:, 6, :], ACT.Copy).then_inc(o_hi, 1)

            def hybrid_part(what, k):
                if what == "square":
                    ph = by_name["qkv2"]
                    bk = (ph.n0 + k) % 4
                    act.wait_ge(product_done, ph.n0 + k + 1)
                    if k > 0:
                        act.wait_ge(qk_summed, k)
                    if k == 0:
                        act.wait_ge(col_set, 2)
                    for t in range(2):
                        ins = nc.scalar.activation(acc[:, t, :], ps[:, bk + 4 * t, 0:256], ACT.Square,
                                                   scale=rcol[:, t:t + 1])
                    ins.then_inc(qk_squared, 1)
                elif what == "root":
                    act.wait_ge(qk_summed, k + 1)
                    nc.scalar.activation(small[:, 16:24], small[:, 8:16], ACT.Sqrt, bias=small[:, 0:1],
                                         scale=1.0 / HD).then_inc(qk_rooted, 1)
                elif what == "store":
                    ph = by_name["qkv2"]
                    bk = (ph.n0 + k) % 4
                    act.wait_ge(qk_turned, TURNS + k + 1)
                    act.wait_ge(v_stored, 8 + k + 1)
                    if k == 0:
                        act.wait_ge(zeroed, 4)
                    for t in range(2):
                        c, bank = slice(t * P, (t + 1) * P), bk + 4 * t
                        nc.scalar.activation(qT2[:, k, c], ps[:, bank, 0:P], ACT.Copy)
                        for hh in range(2):
                            r = slice(hh * HD, (hh + 1) * HD)
                            ins = nc.scalar.activation(kT2[r, hh, k, c], ps[r, bank, P:2 * P], ACT.Copy)
                    ins.then_inc(emptied[bk], 1)
                elif what == "exp":
                    softmax_exp(prob2, (slice(0, P), slice(P, 384)), HEADS + k)
                elif what == "turned":
                    act.wait_ge(prob_turned, HEADS + k + 1)
                    nc.scalar.activation(probT2[:], flat[:, 2560:2560 + 384], ACT.Copy).then_inc(prob_stored, 1)
                else:
                    act.wait_ge(head_done, HEADS + 2 * k + 2)
                    nc.scalar.activation(t_hi[:, k, :], ps[:, 6, 0:T], ACT.Copy).then_inc(o_hi, 1)

            def hybrid_step(hd):
                if hd > 0:
                    hybrid_part("turned", hd - 1)
                if hd < 8:
                    hybrid_part("exp", hd)
                if hd > 0 and hd % 2 == 0:
                    hybrid_part("output", hd // 2 - 1)

            def sigmoid(c):
                for k in (2 * c, 2 * c + 1, 8 + 2 * c, 9 + 2 * c):
                    ins = nc.scalar.activation(gates[:, k, :], gates[:, k, :], ACT.Sigmoid, bias=v("b_gate_2", k))
                ins.then_inc(gates_set, 1)

            def emit(ph):
                name = ph.name
                if name == "conv_in":
                    for l in range(ph.count):
                        i, r, s = l // 3, l % 3, (ph.n0 + l) % 4
                        if r == 0:
                            act.wait_ge(product_done, l + 1)
                            if i >= 2:
                                wait_emptied(act, ph, (l - 5) % 4, (l - 5) // 4)
                            nc.scalar.activation(flat2(gate[:, i % 2]), ps[:, s, :], ACT.Copy)\
                                .then_inc(emptied[s], 1)
                        if l == 5:
                            act.wait_ge(angle_set, 1)
                            nc.scalar.activation(sin[:], turns[:], ACT.Sin).then_inc(table_set, 1)
                            nc.scalar.activation(cos[:], ang[:], ACT.Sin).then_inc(table_set, 1)
                        if r == 2:
                            wait_emptied(act, ph, l % 4, l // 4)
                            nc.scalar.activation(a_hi[:, 2 * i:2 * i + 2, :], mid[:, i % 2], ACT.Copy)\
                                .then_inc(mid_hi, 1)
                        ahead(ph, l % 4, l // 4, split, 3)
                elif name in ("up0", "up1"):
                    run(act, ph, up_body(ph))
                elif name == "up2":
                    run(act, ph, up_conv_body(ph), peel=1)
                    last_high(ph, 10)
                elif name in ycount:
                    if name == "w_o":
                        act.wait_ge(o_split, KD)
                    if name != "w_o":
                        warm(after[name])
                    if name != "w_o":
                        ahead(ph, 0, 0, split, 3)
                    for l in range(ph.count):
                        collect(ph, l % 4, l // 4)
                        if 0 < l < ph.count - 1 and not (name == "w_o" and l == 2):
                            ahead(ph, l % 4, l // 4, split, 3)
                elif name == "qkv":
                    attn_step(0, True, False)
                    with act.Fori(1, 7) as i:
                        attn_step(i, True, True)
                    attn_step(7, True, True, last=True)
                    attn_step(8, False, True)
                elif name == "qkv2":
                    for r in range(4):
                        hybrid_part("square", r)
                        hybrid_part("root", r)
                        if r == 1:
                            act.wait_ge(pooled, 1)
                            nc.scalar.activation(t_hi[:], u_pad[:, :, 16:], ACT.Copy).then_inc(pool_hi, 1)
                        ahead(ph, r, 0, split, 3)
                        if r > 0:
                            hybrid_part("store", r - 1)
                elif name == "pool_in":
                    for l in range(2):
                        ahead(ph, l, 0, split, 3)
                elif name == "gates_a":
                    for l in range(2):
                        if l == 0:
                            hybrid_part("store", 3)
                        hybrid_step(l)
                        ahead(ph, l, 0, split, 3)
                elif name == "w_pool":
                    act.wait_ge(product_done, ph.n0 + 1)
                    for g in range(4):
                        ins = nc.scalar.activation(
                            p_hi[:, g, :], ps[:, ph.n0 % 4 if g < 2 else 7, g % 2 * T:(g % 2 + 1) * T],
                            ACT.Identity, scale=v("pool_scale_2", g))
                    ins.then_inc(pool2_hi, 1)
                    ahead(ph, 0, 0, split, 3)
                elif name == "gates_b":
                    for l in range(ph.count):
                        hybrid_step(l + 2)
                        ahead(ph, l % 4, l // 4, split, 3)
                    hybrid_step(8)
                elif name == "branches":
                    for l in (2, 3, 4, 5):
                        wait_emptied(act, by_name["gates_b"], l % 4, l // 4)
                    sigmoid(0)
                    for j in range(4):
                        ahead(ph, j, 0, split, 3)
                        if j < 3:
                            sigmoid(j + 1)
                        act.wait_ge(mid_ready, j + 1)
                        nc.scalar.activation(mix_hi[:, 2 * j:2 * j + 2, :], mid[:, j % 2], ACT.Copy).then_inc(mid_hi, 1)
                elif name == "w_out2":
                    warm(5)
                    ahead(ph, 0, 0, split, 3)
                    for l in range(ph.count):
                        wait_emptied(act, ph, l, 0)
                        for k in (2 * l, 2 * l + 1):
                            high(5, 0, k)
                            square(k)
                        if l > 0:
                            ahead(ph, l, 0, split, 3)
                elif name == "down2":
                    for l in range(ph.count):
                        ahead(ph, l % 4, l // 4, split, 3)

            for ph, bi in order():
                if ph is not None:
                    emit(ph)
                    if bi is not None:
                        boundary(bi, ph)
            act.wait_ge(turned_out, 1)
            for t in range(2):
                ins = nc.scalar.activation(out_tok[:, t, 0:512], ps[:, 4 + 2 * t, :], ACT.Copy)
            ins.then_inc(out_set, 1)
            act.wait_ge(turned_out, 2)
            nc.scalar.activation(out_tok[:, 0, 512:1024], ps[:, 5, :], ACT.Copy).then_inc(out_set, 1)

        @block.vector
        def _(dve):
            link = Chain(dve, v_seq)

            def split(ph, j, i):
                n, s, r = ph.n(j, i), (ph.n0 + j) % 4, (ph.n0 + j) % 2
                two = ph.empty_last and j == 2
                dve.wait_ge(hi_ready, n + (2 if two else 1))
                size = ph.kt * ph.cols
                nc.vector.tensor_tensor(w_lo[:, s, 0:size], raw[:, r, 0:size], w_hi[:, s, 0:size], ALU.subtract)\
                    .then_inc(lo_ready, 2 if two else 1)

            def low(bi, r, k):
                name, c = bounds[bi][1][r]
                hi, lo = (m_hi, m_lo) if bi == 2 and r == 0 else (x_hi, x_lo)
                dve.wait_ge(norm_hi, norm0[bi] + r * KD + k + 1)
                nc.vector.scalar_tensor_tensor(out=lo[:, k, :], in0=h[:, k, :], scalar=v(name, c + k),
                                               in1=hi[:, k, :], op0=ALU.mult, op1=ALU.subtract)\
                    .then_inc(norm_split, 1)

            def invert(bi):
                dve.wait_ge(rooted, sum0[bi] + (2 if bounds[bi][0] else 1))
                if bi in (2, 4):
                    nc.vector.reciprocal(rcol, small[:, 48:50]).then_inc(col_set, 1)
                if bi != 2:
                    link(nc.vector.reciprocal(rstd[:], rstd[:]))
                if bi == 0:
                    link(nc.vector.tensor_tensor(r_sq[:], rstd[:], rstd[:], ALU.mult))
                if bi == 2:
                    dve.wait_ge(col_set, 1)
                    dve.wait_ge(table_set, 2)
                    for t in range(2):
                        nc.vector.tensor_scalar(cos[:, t, :], cos[:, t, :], rcol[:, t:t + 1], None, ALU.mult)
                        ins = nc.vector.tensor_scalar(sin[:, t, :], sin[:, t, :], rcol[:, t:t + 1], None, ALU.mult)
                    link(ins)

            def boundary(bi, prev):
                if bounds[bi][0]:
                    if bi != 3:
                        ahead(prev, (prev.count - 1) % 4, (prev.count - 1) // 4, split, 2)
                    dve.wait_ge(rooted, sum0[bi] + 1)
                    link(nc.vector.reciprocal(rstd[:], rstd[:]))
                    name, c = bounds[bi][0]
                    for e_ in range(KD):
                        ins = nc.vector.scalar_tensor_tensor(out=y[:, e_, :], in0=y[:, e_, :],
                                                             scalar=v(name, c + e_), in1=rstd[:],
                                                             op0=ALU.mult, op1=ALU.mult)
                        if e_ in pool_tiles:
                            ins.then_inc(y_scaled, 1)
                        else:
                            link(ins)
                            nc.vector.tensor_tensor(h[:, e_, :], h[:, e_, :], y[:, e_, :], ALU.add)\
                                .then_inc(h_added_v, 1)
                    for k in range(KD):
                        low(bi, 0, k)
                    if bi == 2:
                        for k in range(KD):
                            low(bi, 1, k)
                    if bi == 3:
                        ahead(prev, (prev.count - 1) % 4, (prev.count - 1) // 4, split, 2)
                invert(bi)

            def collect(ph, j, i):
                c = 4 * i + j
                if c == ph.count - 1:
                    return
                dve.wait_ge(y_squared, ycount[ph.name] + c + 1)
                dst, src = (acc[:, 0, :], sq[:, 0, :]) if ph.cols == P else (flat2(acc[:]), flat2(sq[:]))
                if c == 0:
                    nc.vector.tensor_copy(dst, src).then_inc(acc_done, 1)
                else:
                    dve.wait_ge(acc_done, ycount[ph.name] + c - after[ph.name] + 1)
                    nc.vector.tensor_tensor(dst, dst, src, ALU.add).then_inc(acc_done, 1)

            n_first = sum(n for _, n in VECS[0])
            n_vec = sum(n for g in VECS for _, n in g)
            dve.wait_ge(turned_in, 1)
            nc.vector.tensor_copy(vec[:, 0:n_first], ps[:, 5, 0:n_first]).then_inc(vec_set, 1)
            for k2 in range(4):
                dve.wait_ge(turned_in, 2 * k2 + 3)
                nc.vector.tensor_copy(flat2(h[:, 2 * k2:2 * k2 + 2, :]), ps[:, k2, :]).then_inc(h_set, 1)
                if k2 == 2:
                    split(*next_chunk(phases[0], 0))
            dve.wait_ge(h_set, 4)
            dve.wait_ge(vec_set, 1)
            for k in range(KD):
                low(0, 0, k)
            split(*next_chunk(phases[0], 1))
            invert(0)

            def angles():
                dve.wait_ge(const_in, N_CONST)
                link(nc.vector.tensor_copy(pos_f[:], pos_i[:]))
                for t in range(2):
                    ins = nc.vector.tensor_scalar(ang[:, t, :], invf[:], pos_f[:, t:t + 1], None, ALU.mult)
                link(ins)
                link(nc.vector.tensor_scalar(turns[:], ang[:], 1.0 / (2 * np.pi), ROUND, ALU.mult, ALU.add))
                link(nc.vector.tensor_scalar(turns[:], turns[:], ROUND, None, ALU.subtract))
                for part in TWO_PI_PARTS:
                    link(nc.vector.scalar_tensor_tensor(out=ang[:], in0=turns[:], scalar=-part, in1=ang[:],
                                                        op0=ALU.mult, op1=ALU.add))
                link(nc.vector.tensor_scalar(turns[:], ang[:], PI_SAFE, -PI_SAFE, ALU.min, ALU.max))
                link(nc.vector.tensor_scalar(ang[:], ang[:], float(np.pi / 2), None, ALU.add))
                link(nc.vector.tensor_scalar(wrap[:], ang[:], float(np.pi), -2 * float(np.pi), ALU.is_gt, ALU.mult))
                link(nc.vector.tensor_tensor(ang[:], ang[:], wrap[:], ALU.add))
                nc.vector.tensor_scalar(ang[:], ang[:], PI_SAFE, -PI_SAFE, ALU.min, ALU.max).then_inc(angle_set, 1)

            def up_body(ph):
                u0 = unit0[ph.name]

                def body(j, i):
                    s, half = (ph.n0 + j) % 4, j // 2
                    u = i * 2 + (u0 + half)
                    dve.wait_ge(product_done, ph.n(j, i) + 1)
                    if j % 2 == 0:
                        wait_emptied(dve, ph, j, i, back=1)
                        nc.vector.tensor_tensor(gate[:, half], ps[:, s, :].rearrange("p (m t) -> p m t", m=2),
                                                by_token(rstd), ALU.mult).then_inc(emptied[s], 1)
                    else:
                        dve.wait_ge(gate_ready, u - 3)
                        dve.wait_ge(mid_split, u - 1)
                        nc.vector.tensor_tensor(flat2(mid[:, half]), ps[:, s, :], flat2(gate[:, half]), ALU.mult)\
                            .then_inc(emptied[s], 1)
                    ahead(ph, j, i, split, 2)
                return body

            def up_conv_body(ph):
                def body(j, i):
                    first = isinstance(i, int) and i == 0 and j < 2
                    s = (ph.n0 + j) % 4
                    dve.wait_ge(product_done, ph.n(j, i) + 1)
                    if not first:
                        dve.wait_ge(taps_done, i * 4 + (j - 1))
                    nc.vector.tensor_tensor(scaled[:, j % 2], ps[:, s, :].rearrange("p (m t) -> p m t", m=2),
                                            by_token(rstd), ALU.mult).then_inc(emptied[s], 1)
                    ahead(ph, j, i, split, 2)
                    dve.wait_ge(conv_base, i * 4 + (j + 1))
                    wait_emptied(dve, ph, j, i)
                    for back in (1, 2):
                        for m in range(2):
                            f = i * 4 + (j // 2 * 2 + j % 2 * KF + m + (2 - back) * 2 * KF)
                            o = gate[:, j % 2, m, back:T]
                            ins = nc.vector.scalar_tensor_tensor(
                                out=o, in0=scaled[:, j % 2, m, 0:T - back],
                                scalar=vec[:, ds(f + col["conv_w_2_01"], 1)], in1=o, op0=ALU.mult, op1=ALU.add)
                        if back == 1:
                            link(ins)
                    ins.then_inc(taps_done, 1)
                return body

            def masked_max(src, mask, parts, c):
                dve.wait_ge(scored, c + 1)
                if not isinstance(c, int):
                    nc.vector.memset(small[:, 40:41], 0.0)
                for t, (cols, ps0) in enumerate(parts):
                    w = cols.stop - cols.start
                    ins = nc.vector.tensor_tensor_reduce(src[:, cols], flat[:, ps0:ps0 + w], mask[:, cols], 1.0,
                                                         -3.0e38, ALU.add, ALU.max, small[:, 2 + t:3 + t])
                link(ins)
                nc.vector.tensor_scalar(small[:, 4:6], small[:, 2:4], -QSCALE, None, ALU.mult).then_inc(max_set, 1)

            def normalise(src, spans, c):
                dve.wait_ge(exped, c * 2 + 2)
                link(nc.vector.reciprocal(small[:, 10:12], small[:, 6:8]))
                for t, cols in enumerate(spans):
                    ins = nc.vector.tensor_scalar(src[:, cols], src[:, cols], small[:, 10 + t:11 + t], None, ALU.mult)
                ins.then_inc(prob_set, 1)

            def rope(i, which, banks, level):
                dve.wait_ge(product_done, level)
                if not (isinstance(i, int) and i == 0 and which == 0):
                    dve.wait_ge(roped, i * 2 + which)
                x_ = ps[:, banks[0]:banks[0] + 2, 0:384].rearrange("p t (g c) -> p t g c", c=HD)
                o = rope_a[:, which].rearrange("p t (g c) -> p t g c", c=HD)
                w = rope_b[:].rearrange("p t (g c) -> p t g c", c=HD)
                half = HD // 2

                def table(t, c0, n):
                    return t[:, :, c0:c0 + n].unsqueeze(2).to_broadcast([P, 2, 6, n])
                nc.vector.tensor_tensor(o, x_, table(cos, 0, HD), ALU.mult)
                nc.vector.tensor_tensor(w[:, :, :, 0:half], x_[:, :, :, half:HD], table(sin, 0, half), ALU.mult)
                link(nc.vector.tensor_tensor(w[:, :, :, half:HD], x_[:, :, :, 0:half], table(sin, half, half), ALU.mult))
                nc.vector.tensor_tensor(rope_a[:, which], rope_a[:, which], rope_b[:], ALU.add).then_inc(roped, 1)

            def attn_step(i, project, attend, last=False):
                ph, q = by_name["qkv"], i - 1
                parts = ((slice(0, 384), S_AT), (slice(384, 1152), S_AT + 512))
                spans = (slice(0, 384), slice(384, 1152))

                def split_next(j):
                    if last:
                        split(*next_chunk(ph, ph.count + j))
                    else:
                        split(ph, j, i + 1)

                if project:
                    split(ph, 2, i)
                if attend:
                    masked_max(prob, mask3, parts, q * 2)
                    normalise(prob, spans, q * 2)
                if not project:
                    output_low(6, 7)
                    split(by_name["w_o"], 2, 0)
                if project:
                    rope(i, 0, Q_BANKS, ph.n(0, i) + 1)
                    if attend:
                        split_next(0)
                    rope(i, 1, K_BANKS, ph.n(1, i) + 1)
                    if not attend:
                        split_next(0)
                if attend:
                    masked_max(prob, mask3, parts, q * 2 + 1)
                    normalise(prob, spans, q * 2 + 1)
                if project:
                    split_next(1)
                    dve.wait_ge(product_done, ph.n(3, i) + 1)
                    if attend:
                        dve.wait_ge(head_done, q * 2 + 2)
                    for t in range(2):
                        ins = nc.vector.tensor_scalar(v_tok[:, t, :], ps[:, V_BANKS[t], 0:384], rcol[:, t:t + 1],
                                                      None, ALU.mult)
                    ins.then_inc(v_stored, 1)
                if last:
                    output_low(0, 6)
                if not project:
                    split(by_name["w_o"], 3, 0)
                    dve.wait_ge(o_hi, KD)
                    nc.vector.tensor_tensor(x_lo[:, 7, :], ps[:, O_BANK, 256:512], x_hi[:, 7, :], ALU.subtract)\
                        .then_inc(o_split, 1)

            def output_low(k0, k1):
                dve.wait_ge(o_hi, k1)
                nc.vector.tensor_tensor(flat2(x_lo[:, k0:k1, :]), flat2(y[:, k0:k1, :]), flat2(x_hi[:, k0:k1, :]),
                                        ALU.subtract).then_inc(o_split, k1 - k0)

            def hybrid_qkv(r):
                ph = by_name["qkv2"]
                bk = (ph.n0 + r) % 4
                dve.wait_ge(qk_squared, r + 1)
                nc.vector.tensor_reduce(small[:, 8:16], acc[:].rearrange("p t (g c) -> p (t g) c", c=HD), AX.X, ALU.add)\
                    .then_inc(qk_summed, 1)
                dve.wait_ge(qk_rooted, r + 1)
                link(nc.vector.reciprocal(small[:, 24:32], small[:, 16:24]))
                if r > 0:
                    dve.wait_ge(qk_turned, TURNS + r)
                q4 = qk[:].rearrange("p t (g c) -> p t g c", c=HD)
                inv = small[:, 24:32].rearrange("p (t g) -> p t g", t=2)
                link(nc.vector.tensor_tensor(inv, inv, rcol.unsqueeze(2).to_broadcast([P, 2, 4]), ALU.mult))
                inv = inv.unsqueeze(3).to_broadcast([P, 2, 4, HD])
                for t in range(2):
                    ins = nc.vector.tensor_scalar(v2[:, t, r, :], ps[:, bk + 4 * t, 256:384], rcol[:, t:t + 1], None,
                                                  ALU.mult)
                ins.then_inc(v_stored, 1)
                for t in range(2):
                    ins = nc.vector.tensor_tensor(q4[:, t], ps[:, bk + 4 * t, 0:256].rearrange("p (g c) -> p g c", c=HD),
                                                  inv[:, t], ALU.mult)
                link(ins)
                for t in range(2):
                    q3 = qk[:, t, :].rearrange("p (w h c) -> p w h c", w=2, h=2)
                    ins = nc.vector.tensor_tensor(q3, q3, g_qk[:].unsqueeze(2).to_broadcast([P, 2, 2, HD]), ALU.mult)
                link(ins)

                def table(c0, n):
                    return rope2[:, :, c0:c0 + n].unsqueeze(2).to_broadcast([P, 2, 4, n])
                nc.vector.tensor_tensor(turn_a[:], q4[:, :, :, 0:16], table(0, 16), ALU.mult)
                nc.vector.tensor_tensor(turn_b[:, :, :, 0:8], q4[:, :, :, 8:16], table(16, 8), ALU.mult)
                link(nc.vector.tensor_tensor(turn_b[:, :, :, 8:16], q4[:, :, :, 0:8], table(24, 8), ALU.mult))
                nc.vector.tensor_tensor(q4[:, :, :, 0:16], turn_a[:], turn_b[:], ALU.add).then_inc(roped, 1)

            def gate_logits(ph, l, k0):
                s = (ph.n0 + l) % 4
                dve.wait_ge(product_done, ph.n0 + l + 1)
                nc.vector.tensor_tensor(gates[:, k0:k0 + 2, :], ps[:, s, :].rearrange("p (m t) -> p m t", m=2),
                                        by_token(rstd), ALU.mult).then_inc(emptied[s], 1)

            def head_front(hd):
                masked_max(prob2, mask1, ((slice(0, P), 4 * 512), (slice(P, 384), 4 * 512 + P)), HEADS + hd)
                normalise(prob2, (slice(0, P), slice(P, 384)), HEADS + hd)

            def hybrid_step(hd):
                if hd < 8:
                    head_front(hd)
                if hd > 0 and hd % 2 == 0:
                    head_out(hd // 2 - 1)

            def head_out(r):
                dve.wait_ge(o_hi, 8 + r + 1)
                nc.vector.tensor_tensor(t_lo[:, r, :], ps[:, 6, 0:T], t_hi[:, r, :], ALU.subtract).then_inc(o_split, 1)

            def emit(ph):
                name = ph.name
                if name == "conv_in":
                    for l in range(ph.count):
                        i, r, s = l // 3, l % 3, (ph.n0 + l) % 4
                        if r == 1:
                            wait_emptied(dve, ph, (l - 1) % 4, (l - 1) // 4)
                            dve.wait_ge(product_done, l + 1)
                            if i == 0:
                                dve.wait_ge(zeroed, 1)
                            nc.vector.tensor_tensor(up[:, :, 2:], ps[:, s, :].rearrange("p (m t) -> p m t", m=2),
                                                    gate[:, i % 2], ALU.mult).then_inc(emptied[s], 1)
                            wait_emptied(dve, ph, l % 4, l // 4)
                            nc.vector.tensor_tensor(up[:, :, 2:], up[:, :, 2:], by_token(r_sq), ALU.mult)\
                                .then_inc(up_set, 1)
                            ahead(ph, l % 4, l // 4, split, 2)
                            dve.wait_ge(up_set, i + 1)
                            for m in range(2):
                                ins = nc.vector.tensor_scalar(cv[:, m, :], up[:, m, 2:], v("conv_w", 16 + 2 * i + m),
                                                              None, ALU.mult)
                            link(ins)
                            for tap in (1, 0):
                                for m in range(2):
                                    ins = nc.vector.scalar_tensor_tensor(
                                        out=cv[:, m, :], in0=up[:, m, tap:tap + T],
                                        scalar=v("conv_w", 8 * tap + 2 * i + m), in1=cv[:, m, :],
                                        op0=ALU.mult, op1=ALU.add)
                                link(ins)
                            link(nc.vector.tensor_tensor(cv[:], cv[:], by_token(rstd), ALU.mult))
                        if l == 3:
                            dve.wait_ge(turned_in, KD + 2)
                            nc.vector.tensor_copy(vec[:, n_first:n_vec], ps[:, 5, n_first:n_vec])\
                                .then_inc(vec_set, 1)
                            angles()
                        if r == 2:
                            dve.wait_ge(product_done, l + 1)
                            if i >= 2:
                                dve.wait_ge(mid_split, i - 1)
                            nc.vector.tensor_tensor(flat2(mid[:, i % 2]), ps[:, s, :], flat2(cv[:]), ALU.mult)\
                                .then_inc(emptied[s], 1)
                        if r != 1:
                            ahead(ph, l % 4, l // 4, split, 2)
                elif name in ("up0", "up1"):
                    run(dve, ph, up_body(ph))
                elif name == "up2":
                    run(dve, ph, up_conv_body(ph), link, 4, peel=1)
                elif name in ycount:
                    if name != "w_o":
                        for l in range(2):
                            ahead(ph, l, 0, split, 2)
                    for l in range(ph.count):
                        collect(ph, l % 4, l // 4)
                        if 1 < l < ph.count - 1:
                            ahead(ph, l % 4, l // 4, split, 2)
                elif name == "qkv":
                    attn_step(0, True, False)
                    with dve.Fori(1, 7) as i:
                        link.enter(i, 6, first=1)
                        attn_step(i, True, True)
                        link.leave(6)
                    attn_step(7, True, True, last=True)
                    attn_step(8, False, True)
                elif name == "qkv2":
                    dve.wait_ge(hybrid_in, 5 * 16)
                    for r in range(4):
                        hybrid_qkv(r)
                        ahead(ph, r, 0, split, 2)
                elif name == "pool_in":
                    for l in range(2):
                        ahead(ph, l, 0, split, 2)
                        s = (ph.n0 + l) % 4
                        dve.wait_ge(product_done, ph.n0 + l + 1)
                        if l == 0:
                            dve.wait_ge(zeroed, 3)
                        nc.vector.tensor_tensor(u_pad[:, 2 * l:2 * l + 2, 16:],
                                                ps[:, s, :].rearrange("p (m t) -> p m t", m=2), by_token(rstd),
                                                ALU.mult).then_inc(emptied[s], 1)
                elif name == "gates_a":
                    for l in range(2):
                        if l == 0:
                            dve.wait_ge(pool_split, 1)
                        gate_logits(ph, l, 2 * l)
                        ahead(ph, l, 0, split, 2)
                        hybrid_step(l)
                elif name == "w_pool":
                    ahead(ph, 0, 0, split, 2)
                    dve.wait_ge(pool2_hi, 1)
                    for g in range(4):
                        ins = nc.vector.scalar_tensor_tensor(
                            out=p_lo[:, g, :], in0=ps[:, ph.n0 % 4 if g < 2 else 7, g % 2 * T:(g % 2 + 1) * T],
                            scalar=v("pool_scale_2", g), in1=p_hi[:, g, :], op0=ALU.mult, op1=ALU.subtract)
                    ins.then_inc(emptied[ph.n0 % 4], 1)
                elif name == "gates_b":
                    for l in range(ph.count):
                        gate_logits(ph, l, 4 + 2 * l)
                        ahead(ph, l % 4, l // 4, split, 2)
                        hybrid_step(l + 2)
                    hybrid_step(8)
                elif name == "branches":
                    for j in range(4):
                        ahead(ph, j, 0, split, 2)
                        s = (ph.n0 + j) % 4
                        dve.wait_ge(product_done, ph.n0 + j + 1)
                        dve.wait_ge(gates_set, j + 1)
                        if j >= 2:
                            dve.wait_ge(mid_split, unit0["branches"] + j - 1)
                        nc.vector.tensor_tensor(flat2(mid[:, j % 2]), ps[:, s, :], flat2(gates[:, 2 * j:2 * j + 2, :]),
                                                ALU.mult)
                        nc.vector.tensor_tensor(flat2(gate[:, j % 2]), ps[:, 4 + s, :],
                                                flat2(gates[:, 8 + 2 * j:10 + 2 * j, :]), ALU.mult)\
                            .then_inc(emptied[s], 1)
                        wait_emptied(dve, ph, j, 0)
                        nc.vector.tensor_tensor(flat2(mid[:, j % 2]), flat2(mid[:, j % 2]), flat2(gate[:, j % 2]),
                                                ALU.add).then_inc(mid_ready, 1)
                elif name in ("w_out2", "down2"):
                    n = ph.cols // P
                    for l in range(2):
                        ahead(ph, l, 0, split, 2)
                    for l in range(ph.count):
                        s = (ph.n0 + l) % 4
                        dve.wait_ge(product_done, ph.n0 + l + 1)
                        h_ = flat2(h[:, n * l:n * l + n, :])
                        nc.vector.tensor_tensor(h_, h_, ps[:, s, 0:n * T], ALU.add).then_inc(emptied[s], 1)
                        if name == "w_out2":
                            wait_emptied(dve, ph, l, 0)
                            for k in (2 * l, 2 * l + 1):
                                low(5, 0, k)
                        if l > 1:
                            ahead(ph, l % 4, l // 4, split, 2)

            for ph, bi in order():
                if ph is not None:
                    emit(ph)
                    if bi is not None:
                        boundary(bi, ph)

            dve.wait_ge(turned_out, 2)
            nc.vector.tensor_copy(out_tok[:, 1, 512:1024], ps[:, 7, :]).then_inc(out_set_v, 1)

        @block.gpsimd
        def _(pool):
            step = Chain(pool, p_seq)
            nc.gpsimd.memset(ones[:], 1.0).then_inc(consts_set, 1)
            nc.gpsimd.memset(small[:], EPS).then_inc(consts_set, 1)
            def hidden_low(hi, lo, u, k0, half):
                pool.wait_ge(mid_hi, u + 1)
                nc.gpsimd.tensor_tensor(lo[:, ds(k0, 2), :], mid[:, half], hi[:, ds(k0, 2), :], ALU.subtract)\
                    .then_inc(mid_split, 1)

            def unit(name, i, half):
                u = i * 2 + (unit0[name] + half)
                pool.wait_ge(silu_done, u - 3)
                nc.gpsimd.tensor_tensor(gate[:, half], gate[:, half], by_token(rstd), ALU.mult)\
                    .then_inc(gate_ready, 1)
                hidden_low(a_hi, a_lo, u, i * 4 + 2 * half, half)

            def last_unit(i, half):
                u = i * 2 + half
                pool.wait_ge(silu_done, u + 23)
                pool.wait_ge(taps_done, u * 2 + 2)
                pool.wait_ge(mid_split, u + unit0["up2"])
                nc.gpsimd.tensor_tensor(flat2(mid[:, 0]), flat2(gate[:, 0]), flat2(gate[:, 1]), ALU.mult)\
                    .then_inc(mid_ready, 1)
                hidden_low(a_hi, a_lo, u + unit0["up2"], u * 2, 0)

            def pool_windows():
                W = T + 16
                s2, s4, s8, s16 = s_win
                step(nc.gpsimd.tensor_tensor(s2[:, :, 1:W], u_pad[:, :, 1:W], u_pad[:, :, 0:W - 1], ALU.add))
                step(nc.gpsimd.tensor_tensor(s4[:, :, 3:W], s2[:, 1:4, 3:W], s2[:, 1:4, 1:W - 2], ALU.add))
                step(nc.gpsimd.tensor_tensor(s8[:, :, 7:W], s4[:, 1:3, 7:W], s4[:, 1:3, 3:W - 4], ALU.add))
                step(nc.gpsimd.tensor_tensor(s16[:, :, 15:W], s8[:, 1:2, 15:W], s8[:, 1:2, 7:W - 8], ALU.add))
                for g in range(4):
                    ins = nc.gpsimd.tensor_tensor(fix[:, g, :], s_win[g][:, 0, 16:32], rcount[:, g, :], ALU.mult)
                step(ins)
                step(nc.gpsimd.tensor_tensor(fix[:], fix[:], u_pad[:, :, 16:32], ALU.subtract))
                for g in range(4):
                    ins = nc.gpsimd.tensor_scalar(s_win[g][:, 0, 16:W], s_win[g][:, 0, 16:W], 1.0 / POOL_WINDOWS[g],
                                                  None, ALU.mult)
                step(ins)
                for g in range(4):
                    ins = nc.gpsimd.tensor_tensor(u_pad[:, g, 16:W], s_win[g][:, 0, 16:W], u_pad[:, g, 16:W],
                                                  ALU.subtract)
                step(ins)
                nc.gpsimd.tensor_copy(u_pad[:, :, 16:32], fix[:]).then_inc(pooled, 1)

            def pair_squares(bi, e_):
                pool.wait_ge(squared, sq0[bi] + 2 * e_ + 2)
                nc.gpsimd.tensor_tensor(y[:, 2 * e_, :], y[:, 2 * e_, :], y[:, 2 * e_ + 1, :], ALU.add)\
                    .then_inc(paired, 1)

            for e_ in range(KD // 2):
                pair_squares(0, e_)
            pool.wait_ge(turned_in, KD + 2)
            nc.gpsimd.memset(up[:, :, 0:2], 0.0).then_inc(zeroed, 1)
            for ph, bi in order():
                if ph is not None:
                    name = ph.name
                    if name == "w_out2":
                        for e_ in range(KD // 2):
                            pair_squares(5, e_)
                    if name == "conv_in":
                        for i in range(4):
                            hidden_low(a_hi, a_lo, i, 2 * i, i % 2)
                    elif name in ("up0", "up1"):
                        with pool.Fori(0, 5) as i:
                            for half in range(2):
                                unit(name, i, half)
                        unit(name, 5, 0)
                    elif name == "up2":
                        last_unit(0, 0)
                        last_unit(0, 1)
                        with pool.Fori(1, 5) as i:
                            for half in range(2):
                                last_unit(i, half)
                        last_unit(5, 0)
                    elif name == "branches":
                        for j in range(4):
                            pool.wait_ge(mid_hi, unit0[name] + j + 1)
                            nc.gpsimd.tensor_tensor(mix_lo[j // 2][:, j % 2 * 2:j % 2 * 2 + 2, :], mid[:, j % 2],
                                                    mix_hi[:, 2 * j:2 * j + 2, :], ALU.subtract).then_inc(mid_split, 1)
                    elif name == "qkv":
                        pool.wait_ge(product_done, ph.n0)
                        nc.gpsimd.memset(kT[:], 0.0).then_inc(zeroed, 1)
                    elif name == "pool_in":
                        pool.wait_ge(product_done, ph.n0)
                        nc.gpsimd.memset(u_pad[:, :, 0:16], 0.0).then_inc(zeroed, 1)
                        nc.gpsimd.memset(kT2[:], 0.0).then_inc(zeroed, 1)
                        pool.wait_ge(hybrid_in, 5 * 16)
                        for l in range(2):
                            wait_emptied(pool, ph, l, 0)
                        pool_windows()
                        pool.wait_ge(pool_hi, 1)
                        nc.gpsimd.tensor_tensor(t_lo[:], u_pad[:, :, 16:], t_hi[:], ALU.subtract)\
                            .then_inc(pool_split, 1)
                if bi is not None and bounds[bi][0]:
                    for e_, k in enumerate(pool_tiles):
                        pool.wait_ge(y_scaled, add0[bi] * len(pool_tiles) + e_ + 1)
                        nc.gpsimd.tensor_tensor(h[:, k, :], h[:, k, :], y[:, k, :], ALU.add).then_inc(h_added_g, 1)
                        pair_squares(bi, e_)
                    pair_squares(bi, 3)


def constants():
    q, k = np.arange(T)[:, None], np.arange(T)[None, :]

    def additive(ok):
        m = np.where(ok, 0.0, NEG).astype(np.float32)
        return m[0:P, 0:P], m[P:T, 0:T]

    parts = [additive((k <= q) & (q - k <= w) & ((q - k) % d == 0)) for w, d in BRANCHES]
    mask3 = np.concatenate([p[0] for p in parts] + [p[1] for p in parts], axis=1)
    mask1 = np.concatenate(additive(k <= q), axis=1)
    half = HD // 2
    f = (np.float32(10000.0) ** (-np.arange(half, dtype=np.float32) / np.float32(half))).astype(np.float32)
    invf = np.broadcast_to(np.concatenate([-f, f]), (P, HD)).copy()
    r = HD // 8
    f2 = (np.float32(500000.0) ** (-np.arange(r, dtype=np.float32) / np.float32(r))).astype(np.float32)
    ang = (np.arange(T, dtype=np.float32)[:, None] * f2[None, :]).astype(np.float32)
    c, s = np.cos(ang), np.sin(ang)
    rope2 = np.concatenate([c, c, -s, s], axis=1).astype(np.float32).reshape(2, P, 4 * r).transpose(1, 0, 2).copy()
    t = np.arange(16)
    rc = np.stack([1.0 / np.minimum(t + 1.0, w) for w in POOL_WINDOWS]).astype(np.float32)
    bf16 = mybir.dt.np(BF16)
    return {"c_ident": np.eye(P, dtype=np.float32), "c_mask3": mask3.astype(bf16), "c_mask1": mask1.astype(bf16),
            "c_invf": invf, "c_rope2": rope2, "c_rcount": np.broadcast_to(rc, (P, 4, 16)).copy()}


_INS = ["x", "positions", "mix_norm_pre", "mix_norm_post", "ffn_norm_pre", "ffn_norm_post", "ffn_w_gate_up",
        "ffn_w_down", "conv_w_in", "conv_w", "conv_w_out", "kv_norm", "w_kv", "w_q", "w_o", "norm_mix_g_2", "w_in_2",
        "b_gate_2", "q_norm_g_2", "k_norm_g_2", "w_pool_2", "pool_scale_2", "w_branch_attn_2", "w_branch_pool_2",
        "w_out_2", "norm_ffn_g_2", "w_up_2", "conv_w_2", "conv_b_2", "w_down_2"]


def kernel(**inputs):
    import concourse.bacc as bacc
    from concourse.bass_utils import run_bass_kernel_spmd as launch

    nc = bacc.Bacc("TRN2", target_bir_lowering=False, num_devices=1)
    given = {name: np.ascontiguousarray(inputs[name]) for name in _INS}
    given.update(constants())
    arrays, args = {}, {}
    for name, value in given.items():
        arrays[f"in_{name}"] = value
        args[name] = nc.dram_tensor(f"in_{name}", value.shape, mybir.dt.from_np(value.dtype),
                                    kind="ExternalInput").ap()
    out = nc.dram_tensor("out", (1, T, D), F32, kind="ExternalOutput").ap()
    build(nc, args, out)
    r = launch(nc, [arrays], core_ids=[0])
    return r.results[0]["out"]
```
